# Optimizing a Trainium2 kernel written in Bass

```python
import math
import jax, jax.numpy as jnp
from jax import lax
import numpy as np

D_MODEL = 1024
BATCH = 1
SEQ = 256
DEPTH = 2

CONV_WIDTH = D_MODEL // 2
CONV_HEAD_DIM = 64
N_CONV_HEADS = CONV_WIDTH // CONV_HEAD_DIM
CONV_K = 3
SSM_WIDTH = D_MODEL - CONV_WIDTH
SSM_GROUP = 16
SSM_GROUPS = SSM_WIDTH // SSM_GROUP
SSM_STATE = 64
MIX_WIDTH = CONV_WIDTH + SSM_WIDTH
IN_COLS = 3 * CONV_WIDTH + SSM_WIDTH
D_FF = ((8 * D_MODEL // 3 + 127) // 128) * 128
PLE_DIM = 256
EPS = 1e-6
DT_MIN = 1e-3
DT_MAX = 1e-1

kernel_name = "hymba_style_conv_s5_macaron_trunk"

def rmsnorm(x, g):
    xf = x.astype(jnp.float32)
    xf = xf * lax.rsqrt(jnp.mean(xf * xf, axis=-1, keepdims=True) + EPS)
    return (xf * g.astype(jnp.float32)).astype(x.dtype)

def swiglu(u, w_gate, w_up, w_down):
    return (jax.nn.silu(u @ w_gate) * (u @ w_up)) @ w_down

def short_conv_group(z_b, z_c, z_v, conv_w, conv_b):
    v = z_c * z_v
    rhs = conv_w.astype(v.dtype)[:, None, :]
    y = lax.conv_general_dilated(
        v, rhs, window_strides=(1,), padding=[(CONV_K - 1, 0)],
        dimension_numbers=("NWC", "WIO", "NWC"), feature_group_count=CONV_WIDTH)
    return z_b * (y + conv_b.astype(v.dtype))

def s5_group(u_s, A_re, A_im, B_re, B_im, C_re, C_im, D, log_dt, glu_w, glu_b):
    f32 = jnp.float32
    bsz, L, _ = u_s.shape
    u = u_s.astype(f32).reshape(bsz, L, SSM_GROUPS, SSM_GROUP)
    ar, ai = A_re.astype(f32), A_im.astype(f32)
    dt = jnp.exp(log_dt.astype(f32))[:, None]
    mag = jnp.exp(ar * dt)
    ph = ai * dt
    lb_re, lb_im = mag * jnp.cos(ph), mag * jnp.sin(ph)
    nr, ni = lb_re - 1.0, lb_im
    den = ar * ar + ai * ai
    f_re = (nr * ar + ni * ai) / den
    f_im = (ni * ar - nr * ai) / den
    br, bi = B_re.astype(f32), B_im.astype(f32)
    bb_re = f_re[..., None] * br - f_im[..., None] * bi
    bb_im = f_re[..., None] * bi + f_im[..., None] * br
    bu_re = jnp.einsum("blgh,gph->blgp", u, bb_re)
    bu_im = jnp.einsum("blgh,gph->blgp", u, bb_im)
    a_re = jnp.broadcast_to(lb_re[None, None], (1, L, SSM_GROUPS, SSM_STATE))
    a_im = jnp.broadcast_to(lb_im[None, None], (1, L, SSM_GROUPS, SSM_STATE))

    def combine(e1, e2):
        a1r, a1i, b1r, b1i = e1
        a2r, a2i, b2r, b2i = e2
        return (a1r * a2r - a1i * a2i,
                a1r * a2i + a1i * a2r,
                a2r * b1r - a2i * b1i + b2r,
                a2r * b1i + a2i * b1r + b2i)

    _, _, h_re, h_im = lax.associative_scan(combine, (a_re, a_im, bu_re, bu_im), axis=1)
    y = (jnp.einsum("blgp,ghp->blgh", h_re, C_re.astype(f32))
         - jnp.einsum("blgp,ghp->blgh", h_im, C_im.astype(f32))
         + D.astype(f32) * u)
    y = y.reshape(bsz, L, SSM_WIDTH)
    zg = jax.nn.gelu(y)
    out = zg * jax.nn.sigmoid(zg @ glu_w.astype(f32) + glu_b.astype(f32))
    return out.astype(u_s.dtype)

def setup_inputs(seed: int = 0) -> dict:
    key = jax.random.key(seed)
    ks = iter(jax.random.split(key, 40))
    nrm = lambda shape, s: jax.random.normal(next(ks), shape, jnp.float32) * s
    gain = lambda shape: 1.0 + nrm(shape, 0.02)
    n = jnp.arange(SSM_STATE, dtype=jnp.float32)
    log_dt = jax.random.uniform(next(ks), (DEPTH, SSM_GROUPS), jnp.float32,
                                math.log(DT_MIN), math.log(DT_MAX))
    return {
        "x": nrm((BATCH, SEQ, D_MODEL), 1.0),
        "p": nrm((DEPTH, BATCH, SEQ, PLE_DIM), 1.0),
        "ffn1_norm": gain((DEPTH, D_MODEL)),
        "ffn1_w_gate": nrm((DEPTH, D_MODEL, D_FF), D_MODEL ** -0.5),
        "ffn1_w_up": nrm((DEPTH, D_MODEL, D_FF), D_MODEL ** -0.5),
        "ffn1_w_down": nrm((DEPTH, D_FF, D_MODEL), D_FF ** -0.5),
        "mix_norm": gain((DEPTH, D_MODEL)),
        "w_in": nrm((DEPTH, D_MODEL, IN_COLS), D_MODEL ** -0.5),
        "conv_w": nrm((DEPTH, CONV_K, CONV_WIDTH), CONV_K ** -0.5),
        "conv_b": nrm((DEPTH, CONV_WIDTH), 0.02),
        "ssm_A_re": -0.5 + nrm((DEPTH, SSM_GROUPS, SSM_STATE), 0.01),
        "ssm_A_im": math.pi * n + nrm((DEPTH, SSM_GROUPS, SSM_STATE), 0.01),
        "ssm_B_re": nrm((DEPTH, SSM_GROUPS, SSM_STATE, SSM_GROUP), (2 * SSM_GROUP) ** -0.5),
        "ssm_B_im": nrm((DEPTH, SSM_GROUPS, SSM_STATE, SSM_GROUP), (2 * SSM_GROUP) ** -0.5),
        "ssm_C_re": nrm((DEPTH, SSM_GROUPS, SSM_GROUP, SSM_STATE), (2 * SSM_STATE) ** -0.5),
        "ssm_C_im": nrm((DEPTH, SSM_GROUPS, SSM_GROUP, SSM_STATE), (2 * SSM_STATE) ** -0.5),
        "ssm_D": nrm((DEPTH, SSM_GROUPS, SSM_GROUP), 1.0),
        "ssm_log_dt": log_dt,
        "glu_w": nrm((DEPTH, SSM_WIDTH, SSM_WIDTH), SSM_WIDTH ** -0.5),
        "glu_b": nrm((DEPTH, SSM_WIDTH), 0.02),
        "conv_out_norm": gain((DEPTH, CONV_WIDTH)),
        "ssm_out_norm": gain((DEPTH, SSM_WIDTH)),
        "w_out": nrm((DEPTH, MIX_WIDTH, D_MODEL), MIX_WIDTH ** -0.5),
        "ffn2_norm": gain((DEPTH, D_MODEL)),
        "ffn2_w_gate": nrm((DEPTH, D_MODEL, D_FF), D_MODEL ** -0.5),
        "ffn2_w_up": nrm((DEPTH, D_MODEL, D_FF), D_MODEL ** -0.5),
        "ffn2_w_down": nrm((DEPTH, D_FF, D_MODEL), D_FF ** -0.5),
        "ple_norm": gain((DEPTH, D_MODEL)),
        "ple_w_gate": nrm((DEPTH, D_MODEL, D_MODEL), D_MODEL ** -0.5),
        "ple_w_proj": nrm((DEPTH, PLE_DIM, D_MODEL), PLE_DIM ** -0.5),
        "final_norm": gain((D_MODEL,)),
    }

def reference(x, p, ffn1_norm, ffn1_w_gate, ffn1_w_up, ffn1_w_down, mix_norm, w_in,
              conv_w, conv_b, ssm_A_re, ssm_A_im, ssm_B_re, ssm_B_im, ssm_C_re, ssm_C_im,
              ssm_D, ssm_log_dt, glu_w, glu_b, conv_out_norm, ssm_out_norm, w_out,
              ffn2_norm, ffn2_w_gate, ffn2_w_up, ffn2_w_down, ple_norm, ple_w_gate,
              ple_w_proj, final_norm):
    h = x
    for i in range(DEPTH):
        h = h + 0.5 * swiglu(rmsnorm(h, ffn1_norm[i]), ffn1_w_gate[i], ffn1_w_up[i], ffn1_w_down[i])
        z = rmsnorm(h, mix_norm[i]) @ w_in[i]
        z_b = z[..., :CONV_WIDTH]
        z_c = z[..., CONV_WIDTH:2 * CONV_WIDTH]
        z_v = z[..., 2 * CONV_WIDTH:3 * CONV_WIDTH]
        z_s = z[..., 3 * CONV_WIDTH:]
        y_a = short_conv_group(z_b, z_c, z_v, conv_w[i], conv_b[i])
        y_s = s5_group(z_s, ssm_A_re[i], ssm_A_im[i], ssm_B_re[i], ssm_B_im[i],
                       ssm_C_re[i], ssm_C_im[i], ssm_D[i], ssm_log_dt[i], glu_w[i], glu_b[i])
        y = jnp.concatenate([rmsnorm(y_a, conv_out_norm[i]), rmsnorm(y_s, ssm_out_norm[i])], axis=-1)
        h = h + y @ w_out[i]
        h = h + 0.5 * swiglu(rmsnorm(h, ffn2_norm[i]), ffn2_w_gate[i], ffn2_w_up[i], ffn2_w_down[i])
        gate = jax.nn.sigmoid(rmsnorm(h, ple_norm[i]) @ ple_w_gate[i])
        h = h + (p[i] @ ple_w_proj[i]) * gate
    return rmsnorm(h, final_norm)


_drawn_inputs = setup_inputs


def setup_inputs(seed=0):
    import zlib

    import numpy as np

    out = dict(_drawn_inputs(seed))
    spreads = {}
    factors = {'ffn1_norm': 4.585,
     'conv_b': 4.423,
     'ssm_A_re': 200.0,
     'glu_b': 8.0,
     'conv_out_norm': 19.386,
     'ssm_out_norm': 18.548,
     'ffn2_norm': 7.444,
     'ple_norm': 200.0,
     'final_norm': 21.328,
     'ssm_A_im': 29.952,
     'ssm_B_re': 40.648,
     'ssm_B_im': 41.416,
     'ssm_C_re': 40.936,
     'ssm_C_im': 41.152,
     'ssm_log_dt': 33.232}
    for name, (base, spread) in spreads.items():
        noise = np.random.default_rng([zlib.crc32(name.encode()), seed]).standard_normal(out[name].shape)
        drawn = base * np.exp(spread * noise) if base else spread * noise
        out[name] = __import__('jax').numpy.asarray(drawn.astype(out[name].dtype))
    for name, factor in factors.items():
        out[name] = (out[name] * factor).astype(out[name].dtype)
    return out
```

```python
import math
from contextlib import ExitStack

import concourse.bass as bass
from concourse import mybir

F32 = mybir.dt.float32
F32R = mybir.dt.float32r
I32 = mybir.dt.int32
ALU = mybir.AluOpType
ACT = mybir.ActivationFunctionType

P = 128
D = 1024
SEQ = 256
DEPTH = 2
NT = SEQ // P
KD = D // P
CW = D // 2
NCH = CW // P
FF = 2816
FC = 256
NFC = FF // FC
PLE = 256
EPS = 1e-6
UNIT = 2048
SLOTS = 3

T = 4
NCK = SEQ // T
NB = 16
GRP = 16
ST = 64

U_FFN1 = 0
U_IN = U_FFN1 + 3 * NFC
U_WOUT_A = U_IN + 8
U_GLU = U_WOUT_A + 2
U_WOUT_S = U_GLU + 1
U_FFN2 = U_WOUT_S + 2
U_PROJ = U_FFN2 + 3 * NFC
U_GATE = U_PROJ + 1
UNITS = U_GATE + 4
assert UNITS % SLOTS == 0 and UNITS == 84
IN_COLS = [1536, 1792, 512, 768, 1024, 1280, 0, 256]

V_NORM = [0, 8, 16, 24]
V_CW, V_CB, V_GB, V_GA, V_GS = 32, 44, 48, 52, 56
V_AR, V_AI, V_LDT, V_D = 60, 76, 96, 112

LOG2E = 1.4426950408889634
LN2_HI, LN2_LO = 0.693359375, -2.12194440e-4
ROUND = 12582912.0
TWO_PI_1 = 6.28125
TWO_PI_2 = 0.0019350051879882812
TWO_PI_3 = 2 * math.pi - TWO_PI_1 - TWO_PI_2
GELU_C = math.sqrt(2 / math.pi)

DVE_LINKS = 6
NPV = 14
NBC = 6


def trunk(nc, x, p, ffn1_norm, ffn1_w_gate, ffn1_w_up, ffn1_w_down, mix_norm, w_in, conv_w, conv_b,
          ssm_A_re, ssm_A_im, ssm_B_re, ssm_B_im, ssm_C_re, ssm_C_im, ssm_D, ssm_log_dt, glu_w, glu_b,
          conv_out_norm, ssm_out_norm, w_out, ffn2_norm, ffn2_w_gate, ffn2_w_up, ffn2_w_down,
          ple_norm, ple_w_gate, ple_w_proj, final_norm, out):
    with ExitStack() as ctx:
        def sb(name, shape, dt=F32):
            return ctx.enter_context(nc.sbuf_tensor(name, shape, dt))

        def sem(name):
            return ctx.enter_context(nc.semaphore(name))

        raw = sb("raw", [P, SLOTS, UNIT])
        wH = sb("wH", [P, SLOTS, UNIT], F32R)
        wL = sb("wL", [P, SLOTS, UNIT], F32R)
        xres = sb("xres", [P, NT, D])
        uH = sb("uH", [P, KD, SEQ], F32R)
        uL = sb("uL", [P, KD, SEQ], F32R)
        tg = sb("tg", [P, 2, 512])
        hTH = sb("hTH", [P, 2, SEQ], F32R)
        hTL = sb("hTL", [P, 2, SEQ], F32R)
        pTH = sb("pTH", [P, 2, SEQ], F32R)
        pTL = sb("pTL", [P, 2, SEQ], F32R)
        pvec = sb("pvec", [P, P])
        pvT = sb("pvT", [P, P])
        ldt = sb("ldt", [P, 2])
        hgb = sb("hgb", [P, NCH])
        pnat = sb("pnat", [P, NT, PLE])
        ident = sb("ident", [P, P])
        ones = sb("ones", [P, P])
        rsb = sb("rsb", [P, SEQ])
        rsb2 = sb("rsb2", [P, SEQ])
        ssq = sb("ssq", [P, NT])
        ms = sb("ms", [P, NT])
        rs = sb("rs", [P, NT])
        ms_y = sb("ms_y", [P, 2, NT])
        rs_y = sb("rs_y", [P, 2, NT])
        mhalf = sb("mhalf", [P, NB])
        mone = sb("mone", [P, NB])
        prm = sb("prm", [P, 32, NB])
        prmi = sb("prmi", [P, NB], I32)
        bufB = sb("bufB", [P, 1024])
        sil = bufB[:, 0:512].rearrange("p (t c) -> p t c", t=NT)
        hid = bufB[:, 512:1024].rearrange("p (t c) -> p t c", t=NT)
        u4 = bufB[:, :].rearrange("p (b c) -> p b c", b=NB)
        bufA = sb("bufA", [P, 2048])
        pp = bufA[:, :].rearrange("p (t n) -> p t n", t=NT)
        us = bufA[:, 0:1024].rearrange("p (i n) -> p i n", i=NCH)
        sqy = us
        cy = bufA[:, 1024:2048].rearrange("p (i n) -> p i n", i=NCH)
        vv = sb("vv", [P, NCH, SEQ + 2])
        ctmp = sb("ctmp", [P, SEQ])
        diag = ctmp[:].rearrange("p (t n) -> p t n", t=NT)
        Gr = sb("Gr", [P, NB, T + 1, 32])
        Gi = sb("Gi", [P, NB, T + 1, 32])
        taps = sb("taps", [P, NB, P])
        kc = sb("kc", [P, NB, 32])
        dtmp = pnat[:].rearrange("p t d -> p (t d)").rearrange("p (b c) -> p b c", b=NB)
        cosT = sb("cosT", [P, NB, NCK])
        sinT = sb("sinT", [P, NB, NCK])
        decay = sb("decay", [P, NB, NCK])
        regE = sb("regE", [P, 4096])
        Er = regE[:, 0:2048].rearrange("p (b s c) -> p b s c", b=NB, s=T)
        Ei = regE[:, 2048:4096].rearrange("p (b s c) -> p b s c", b=NB, s=T)
        Sr = regE[:, 0:1024].rearrange("p (b c) -> p b c", b=NB)
        Si = regE[:, 1024:2048].rearrange("p (b c) -> p b c", b=NB)
        zr, zi = regE[:, 2048:2560], regE[:, 2560:3072]
        t1 = regE[:, 3072:4096]
        regT = sb("regT", [P, 4096])
        ETr = regT[:, 0:2048].rearrange("p (b c) -> p b c", b=NB)
        ETi = regT[:, 2048:4096].rearrange("p (b c) -> p b c", b=NB)
        mm = regT[:, 0:2048].rearrange("p (n c) -> p n c", n=4)
        th = regT[:, 2048:3072]
        zgT = regT[:, 3072:4096].rearrange("p (i n) -> p i n", i=NCH)
        cnat = regT[:, 0:1024].rearrange("p (r q d c) -> p r q d c", r=2, q=4, d=2)
        br = regT[:, 1024:1280].rearrange("p (b h) -> p b h", b=NB)
        bi = regT[:, 1280:1536].rearrange("p (b h) -> p b h", b=NB)
        cr = regT[:, 1536:1792].rearrange("p (b h) -> p b h", b=NB)
        nci = regT[:, 1792:2048].rearrange("p (b h) -> p b h", b=NB)
        bbr = regT[:, 2048:2304].rearrange("p (b h) -> p b h", b=NB)
        bbi = regT[:, 2304:2560].rearrange("p (b h) -> p b h", b=NB)
        pa = regT[:, 2560:3072].rearrange("p (b h) -> p b h", b=NB)
        pb = regT[:, 3072:3584].rearrange("p (b h) -> p b h", b=NB)
        ps = ctx.enter_context(nc.psum_tensor("ps", [P, 8, 512], F32))

        usq = us.rearrange("p i (c s) -> p i c s", s=T)
        u4q = bufB[:, :].rearrange("p (i q c) -> p i q c", i=NCH, q=4)
        t1q = t1.rearrange("p (i q c) -> p i q c", i=NCH, q=4)
        zgq = zgT.rearrange("p i (c s) -> p i c s", s=T)
        thv = th.rearrange("p (i n) -> p i n", i=NCH)

        ld = [sem(f"ld{s}") for s in range(SLOTS)]
        wh_done, wl_done, wt_used = sem("wh_done"), sem("wl_done"), sem("wt_used")
        x_ld, vec_ld, bc_ld, fin_ld, stored = (sem(n) for n in ("x_ld", "vec_ld", "bc_ld", "fin_ld", "stored"))
        consts = sem("consts")
        pv_full, pvt_ps, pvt_done = sem("pv_full"), sem("pvt_ps"), sem("pvt_done")
        x_ready = sem("x_ready")
        xt_ps, tg_done, uh_done, ul_done = sem("xt_ps"), sem("tg_done"), sem("uh_done"), sem("ul_done")
        ssq_done, rs_done = sem("ssq_done"), sem("rs_done")
        gu_t0, sil_done, hid_done = sem("gu_t0"), sem("sil_done"), sem("hid_done")
        ht_ps, hh_done, hl_done, acc_t0 = sem("ht_ps"), sem("hh_done"), sem("hl_done"), sem("acc_t0")
        ct_ps, ct_done, pt_ps, pth_done = sem("ct_ps"), sem("ct_done"), sem("pt_ps"), sem("pth_done")
        ptl_done, hgb_done = sem("ptl_done"), sem("hgb_done")
        ssm_ready, et_ps, et_done = sem("ssm_ready"), sem("et_ps"), sem("et_done")
        kc_ps, kc_done, kc_full, taps_done = sem("kc_ps"), sem("kc_done"), sem("kc_full"), sem("taps_done")
        diag_done, rsb_ps, z_out, u4a_done, u4d_done = (
            sem("diag_done"), sem("rsb_ps"), sem("z_out"), sem("u4a_done"), sem("u4d_done"))
        dl_ps, rot_in, zi_done, scan_done, rot_out, s_done, y_ps = (
            sem("dl_ps"), sem("rot_in"), sem("zi_done"), sem("scan_done"), sem("rot_out"), sem("s_done"), sem("y_ps"))
        conv_done, sq_done, st_ps, msy_done, rsy_done = (
            sem("conv_done"), sem("sq_done"), sem("st_ps"), sem("msy_done"), sem("rsy_done"))
        yh_done, yl_done, xa_done = sem("yh_done"), sem("yl_done"), sem("xa_done")
        ysq_done, cub_done, tanh_done, zg_done = sem("ysq_done"), sem("cub_done"), sem("tanh_done"), sem("zg_done")
        zga_done, zgd_done, zgh_done, zgl_done = sem("zga_done"), sem("zgd_done"), sem("zgh_done"), sem("zgl_done")
        glu_h0, th2_done, yy_done = sem("glu_h0"), sem("th2_done"), sem("yy_done")
        pp_done, gate_done, gx_done = sem("pp_done"), sem("gate_done"), sem("gx_done")
        pool_link, dve_link, fin_done, passed = sem("pool_link"), sem("dve_link"), sem("fin_done"), sem("passed")

        PER_SLOT = UNITS // SLOTS
        FFN_BASE = (U_FFN1, U_FFN2)

        def used(l, n):
            return l * UNITS + n + 1 + SLOTS

        block = ctx.enter_context(nc.Block())

        @block.sync
        def _(sp):
            sp.dma_start(xres[:], x[0].rearrange("(t p) d -> p t d", p=P)).then_inc(x_ld, 16)

            def unit(l, n, slot, halves):
                sp.wait_ge(wl_done, l * UNITS + n + 1)
                sp.sem_inc(passed, 1)
                for dst, src in halves:
                    sp.dma_start(dst, src).then_inc(ld[slot], 16)

            def rows(slot, w2d, row):
                v = w2d[bass.ds(row, 2 * P), :].rearrange("(k p) n -> p k n", p=P)
                return [(raw[:, slot, k * D:(k + 1) * D], v[:, k, :]) for k in range(2)]

            def gate_up(slot, wg, wu, col, part):
                dst = raw[:, slot, :].rearrange("p (k g c) -> p k g c", k=4, g=2)
                return [(dst[:, :, g, :], w[part * 512:(part + 1) * 512, bass.ds(col, FC)].rearrange("(k p) c -> p k c", p=P))
                        for g, w in enumerate((wg, wu))]

            def ffn(l, base, wg, wu, wd):
                for part in range(2):
                    slot = (base + part) % SLOTS
                    unit(l, base + part, slot, gate_up(slot, wg, wu, 0, part))
                with sp.Fori(1, NFC) as i:
                    for part in range(2):
                        slot = (base - 1 + part) % SLOTS
                        unit(l, i * 3 + (base - 1 + part), slot, gate_up(slot, wg, wu, i * FC, part))
                    slot = (base + 1) % SLOTS
                    unit(l, i * 3 + (base + 1), slot, rows(slot, wd, (i - 1) * FC))
                n = base + 3 * NFC - 1
                unit(l, n, n % SLOTS, rows(n % SLOTS, wd, (NFC - 1) * FC))

            def at(w, l):
                return w[bass.ds(l, 1)].rearrange("o a b -> (o a) b")

            def vec(w, l):
                return w[bass.ds(l, 1)].rearrange("o (k p) -> (o k) p", p=P)

            sp.wait_ge(consts, 3)
            with sp.Fori(0, DEPTH) as l:
                sp.wait_ge(ptl_done, l + 1)
                sp.sem_inc(passed, 1)
                for row, v in ((V_NORM[0], ffn1_norm), (V_NORM[1], mix_norm), (V_NORM[2], ffn2_norm),
                               (V_NORM[3], ple_norm), (V_CB, conv_b), (V_GB, glu_b), (V_GA, conv_out_norm),
                               (V_GS, ssm_out_norm)):
                    sp.dma_start(pvec[row:row + v.shape[1] // P, :], vec(v, l)).then_inc(vec_ld, 16)
                sp.dma_start(pvec[V_CW:V_CW + 3 * NCH, :],
                             conv_w[bass.ds(l, 1)].rearrange("o j (k p) -> (o j k) p", p=P)).then_inc(vec_ld, 16)
                for row, v in ((V_AR, ssm_A_re), (V_AI, ssm_A_im)):
                    sp.dma_start(pvec[row:row + NB, :], v[bass.ds(l, 1)].rearrange("o (b g) p -> (o b) (g p)", g=2)).then_inc(vec_ld, 16)
                sp.dma_start(ldt[V_LDT:V_LDT + NB, :], ssm_log_dt[bass.ds(l, 1)].rearrange("o (b g) -> (o b) g", g=2)).then_inc(vec_ld, 16)
                sp.dma_start(pvec[V_D:V_D + NB, 96:128], ssm_D[bass.ds(l, 1)].rearrange("o (b g) h -> (o b) (g h)", g=2)).then_inc(vec_ld, 16)
                sp.wait_ge(x_ready, l * 16 + 12)
                sp.sem_inc(passed, 1)
                sp.dma_start(pnat[:], p[bass.ds(l, 1), 0].rearrange("o (t p) d -> p (o t) d", p=P)).then_inc(vec_ld, 16)
                for dst, b in ((br, ssm_B_re), (bi, ssm_B_im)):
                    sp.dma_start(dst, b[bass.ds(l, 1)].rearrange("o (b g) p h -> (g p) (o b) h", g=2)).then_inc(bc_ld, 16)
                for r, c in enumerate((ssm_C_re, ssm_C_im)):
                    for d in range(2):
                        sp.dma_start(cnat[:, r, :, d, :], c[bass.ds(l, 1)].rearrange("o (q g) h p -> (g h) (o q) p", g=8)).then_inc(bc_ld, 16)

                ffn(l, U_FFN1, at(ffn1_w_gate, l), at(ffn1_w_up, l), at(ffn1_w_down, l))
                for j in range(8):
                    n = U_IN + j
                    src = at(w_in, l)[:, IN_COLS[j]:IN_COLS[j] + 256].rearrange("(k p) c -> p k c", p=P)
                    dst = raw[:, n % SLOTS, :].rearrange("p (k c) -> p k c", k=KD)
                    unit(l, n, n % SLOTS, [(dst[:, 4 * a:4 * a + 4, :], src[:, 4 * a:4 * a + 4, :]) for a in range(2)])
                for j in range(2):
                    n = U_WOUT_A + j
                    unit(l, n, n % SLOTS, rows(n % SLOTS, at(w_out, l), j * 2 * P))
                src = at(glu_w, l).rearrange("(k p) c -> p k c", p=P)
                dst = raw[:, U_GLU % SLOTS, :].rearrange("p (k c) -> p k c", k=NCH)
                unit(l, U_GLU, U_GLU % SLOTS, [(dst[:, 2 * a:2 * a + 2, :], src[:, 2 * a:2 * a + 2, :]) for a in range(2)])
                for j in range(2):
                    n = U_WOUT_S + j
                    unit(l, n, n % SLOTS, rows(n % SLOTS, at(w_out, l), CW + j * 2 * P))
                ffn(l, U_FFN2, at(ffn2_w_gate, l), at(ffn2_w_up, l), at(ffn2_w_down, l))
                unit(l, U_PROJ, U_PROJ % SLOTS, rows(U_PROJ % SLOTS, at(ple_w_proj, l), 0))
                for j in range(4):
                    n = U_GATE + j
                    unit(l, n, n % SLOTS, rows(n % SLOTS, at(ple_w_gate, l), j * 2 * P))

            sp.wait_ge(x_ready, DEPTH * 16 + 12)
            sp.dma_start(regT[:, 0:D], final_norm.partition_broadcast(P)).then_inc(fin_ld, 16)
            for t in range(NT):
                sp.wait_ge(fin_done, t + 1)
                sp.dma_start(out[0, t * P:(t + 1) * P, :], xres[:, t, :]).then_inc(stored, 16)
            sp.wait_ge(stored, 16 * NT)

        @block.scalar
        def _(act):
            nc.scalar.preload_act_table_set("silu_and_others")

            def split(l, n, slot, load):
                act.wait_ge(ld[slot], (l * PER_SLOT + load) * 32)
                act.wait_ge(wt_used, l * UNITS + n + 1)
                nc.scalar.activation(wH[:, slot, :], raw[:, slot, :], ACT.Copy).then_inc(wh_done, 1)

            def split_at(l, n):
                split(l, n, n % SLOTS, n // SLOTS + 1)

            def squares(l, m):
                act.wait_ge(x_ready, l * 16 + (16 + 4 * m + 4))
                for t in range(NT):
                    if t == 1:
                        act.wait_ge(ssq_done, l * 8 + (2 * m + 1))
                    nc.scalar.activation(bufB[:, :], xres[:, t, :], ACT.Square,
                                         accum_out=ssq[:, t:t + 1]).then_inc(ssq_done, 1)

            def norm(l, m):
                for q in range(4):
                    t, h = q // 2, q % 2
                    act.wait_ge(tg_done, l * 16 + (4 * m + q + 1))
                    nc.scalar.activation(uH[:, 4 * h:4 * h + 4, t * P:(t + 1) * P],
                                         tg[:, q % 2, :].rearrange("p (k n) -> p k n", k=4),
                                         ACT.Copy).then_inc(uh_done, 1)
                squares(l, m)

            def silus(l, f, i, unit_b):
                for t in range(NT):
                    if t == 0:
                        act.wait_ge(gu_t0, l * (2 * NFC) + i + (f * NFC + 1))
                    else:
                        act.wait_ge(wt_used, used(l, unit_b))
                    nc.scalar.activation(sil[:, t, :], ps[:, t, 0:FC], ACT.Silu,
                                         scale=rs[:, t:t + 1]).then_inc(sil_done, 1)

            def hidden_H(l, f, i):
                act.wait_ge(ht_ps, l * (2 * NFC) + i + (f * NFC + 1))
                nc.scalar.activation(hTH[:], ps[:, 6, :].rearrange("p (k n) -> p k n", k=2),
                                     ACT.Copy).then_inc(hh_done, 1)

            def c_turned(l, r):
                act.wait_ge(ct_ps, l * 2 + (r + 1))
                for g in range(2):
                    src = ps[64 * g:64 * g + 64, 7, :].rearrange("p (b g h) -> p b g h", b=NB, g=2)
                    nc.scalar.activation((cr, nci)[r][64 * g:64 * g + 64], src[:, :, g, :], ACT.Copy,
                                         scale=(1.0, -1.0)[r]).then_inc(ct_done, 1)

            def p_turned(l):
                act.wait_ge(pt_ps, l + 1)
                nc.scalar.activation(pTH[:], ps[:, 7, :].rearrange("p (k n) -> p k n", k=2),
                                     ACT.Copy).then_inc(pth_done, 1)

            def ffn(l, f):
                base = FFN_BASE[f]
                split_at(l, base + 2)
                split_at(l, base + 3)
                act.wait_ge(rs_done, l * 4 + (2 * f + 1))
                silus(l, f, 0, base + 1)
                if f == 0:
                    c_turned(l, 0)
                    c_turned(l, 1)
                    p_turned(l)
                with act.Fori(1, NFC) as i:
                    hidden_H(l, f, i - 1)
                    for part in range(3):
                        if part == 2:
                            silus(l, f, i, i * 3 + base)
                        u = base + 1 + part
                        split(l, i * 3 + u, u % SLOTS, i + (u // SLOTS + 1))
                hidden_H(l, f, NFC - 1)
                split_at(l, base + 3 * NFC + 1)

            def split_y(l, k, gain):
                src = (cy, zgT)[k]
                for i in range(NCH):
                    nc.scalar.activation(uH[:, i, :], src[:, i, :], ACT.Copy,
                                         scale=pvT[:, gain + i:gain + i + 1]).then_inc(yh_done, 1)
                nc.scalar.activation(sqy, src, ACT.Square).then_inc(sq_done, 1)

            def mixer(l):
                split_at(l, U_IN + 2)
                for r in range(2):
                    for b in range(4):
                        act.wait_ge(et_ps, l * 8 + (4 * r + b + 1))
                        nc.scalar.activation((ETr, ETi)[r][:, 4 * b:4 * b + 4, :],
                                             ps[:, 2 + b, :].rearrange("p (b c) -> p b c", b=4),
                                             ACT.Copy).then_inc(et_done, 1)
                    if r == 0:
                        split_at(l, U_IN + 3)
                act.wait_ge(kc_ps, l + 1)
                nc.scalar.activation(kc[:], ps[:, 6, :].rearrange("p (b c) -> p b c", b=NB), ACT.Copy).then_inc(kc_done, 1)
                act.wait_ge(z_out, l * 8 + 2)
                for s in range(2):
                    for q in range(4):
                        nc.scalar.activation(u4q[32 * s:32 * s + 32, :, q, :], usq[32 * q:32 * q + 32, :, :, s],
                                             ACT.Copy).then_inc(u4a_done, 1)
                split_at(l, U_IN + 4)
                split_at(l, U_IN + 5)
                split_at(l, U_IN + 6)
                act.wait_ge(kc_full, l + 1)
                for k in range(T):
                    for s in range(T - k):
                        nc.scalar.activation(taps[32 * s:32 * s + 32, :, 32 * (s + k):32 * (s + k) + 32],
                                             kc[32 * (3 - k):32 * (3 - k) + 32], ACT.Copy).then_inc(taps_done, 1)
                    if k == 0:
                        split_at(l, U_IN + 7)
                split_at(l, U_WOUT_A)
                split_at(l, U_WOUT_A + 1)
                act.wait_ge(z_out, l * 8 + 8)
                split_y(l, 0, V_GA)
                split_at(l, U_GLU)
                for h in range(2):
                    act.wait_ge(y_ps, l * 2 + (h + 1))
                    nc.scalar.activation(t1[:, 512 * h:512 * h + 512], ps[:, 6 + h, :], ACT.Square).then_inc(ysq_done, 1)
                for h in range(2):
                    act.wait_ge(cub_done, l * 2 + (h + 1))
                    nc.scalar.activation(th[:, 512 * h:512 * h + 512], t1[:, 512 * h:512 * h + 512], ACT.Tanh,
                                         scale=GELU_C).then_inc(tanh_done, 1)
                act.wait_ge(zg_done, l * 2 + 2)
                for s in range(2):
                    for q in range(4):
                        nc.scalar.activation(zgq[32 * q:32 * q + 32, :, :, s], t1q[32 * s:32 * s + 32, :, q, :],
                                             ACT.Copy, scale=0.5).then_inc(zga_done, 1)
                act.wait_ge(zga_done, l * 8 + 8)
                act.wait_ge(zgd_done, l * 8 + 8)
                nc.scalar.activation(uH[:, NCH:2 * NCH, :], zgT, ACT.Copy).then_inc(zgh_done, 1)
                split_at(l, U_WOUT_S)
                act.wait_ge(pvt_done, l + 1)
                nc.scalar.activation(hgb[:], pvT[:, V_GB:V_GB + NCH], ACT.Copy, scale=0.5).then_inc(hgb_done, 1)
                split_at(l, U_WOUT_S + 1)
                act.wait_ge(hgb_done, l + 1)
                for i in range(NCH):
                    if i == 0:
                        act.wait_ge(glu_h0, l + 1)
                    if i == 2:
                        act.wait_ge(wt_used, used(l, U_GLU))
                    nc.scalar.activation(thv[:, i, :], ps[:, i // 2, (i % 2) * SEQ:(i % 2 + 1) * SEQ], ACT.Tanh,
                                         bias=hgb[:, i:i + 1], scale=0.5).then_inc(th2_done, 1)
                act.wait_ge(yy_done, l * 2 + 2)
                split_y(l, 1, V_GS)
                split_at(l, U_FFN2)
                split_at(l, U_FFN2 + 1)

            def embedding(l):
                for q in range(4):
                    act.wait_ge(wt_used, used(l, U_PROJ))
                    nc.scalar.activation(pp[:, q // 2, (q % 2) * 512:(q % 2) * 512 + 512],
                                         ps[:, (0, 1, 6, 7)[q], :], ACT.Copy, scale=0.5).then_inc(pp_done, 1)
                norm(l, 3)
                split_at(l, U_GATE + 1)
                split_at(l, U_GATE + 2)
                split_at(l, U_GATE + 3)
                act.wait_ge(rs_done, l * 4 + 4)
                for q in range(4):
                    if q == 0:
                        act.wait_ge(acc_t0, l * 5 + 5)
                    if q == 2:
                        act.wait_ge(wt_used, used(l, U_GATE + 3))
                    if q >= 2:
                        act.wait_ge(gx_done, l * 4 + (q - 1))
                    nc.scalar.activation(bufB[:, (q % 2) * 512:(q % 2) * 512 + 512], ps[:, 2 + q, :], ACT.Tanh,
                                         scale=rs[:, q // 2:q // 2 + 1]).then_inc(gate_done, 1)

            with act.Fori(0, DEPTH) as l:
                act.wait_ge(pvt_ps, l + 1)
                nc.scalar.activation(pvT[:], ps[:, 7, 0:P], ACT.Copy).then_inc(pvt_done, 1)
                split_at(l, 0)
                norm(l, 0)
                split_at(l, 1)
                ffn(l, 0)
                norm(l, 1)
                mixer(l)
                norm(l, 2)
                ffn(l, 1)
                embedding(l)
            squares(DEPTH, 0)

        @block.vector
        def _(dve):
            dve.sem_inc(wl_done, SLOTS)
            dve.sem_inc(ptl_done, 1)
            dve.wait_ge(x_ld, 16)
            dve.sem_inc(x_ready, 20)
            dve.wait_ge(consts, 8)
            links = [0]

            def link(l, ins):
                links[0] += 1
                ins.then_inc(dve_link, 1)
                dve.wait_ge(dve_link, l * DVE_LINKS + links[0])

            def split(l, n, slot):
                dve.wait_ge(wh_done, l * UNITS + n + 1)
                nc.vector.tensor_tensor(wL[:, slot, :], raw[:, slot, :], wH[:, slot, :].bitcast(F32),
                                        ALU.subtract).then_inc(wl_done, 1)

            def split_at(l, n):
                split(l, n, n % SLOTS)

            def norm(l, m):
                def gained(q):
                    h = q % 2
                    dve.wait_ge(xt_ps, l * 16 + (4 * m + q + 1))
                    if q >= 2:
                        dve.wait_ge(ul_done, l * 16 + (4 * m + q - 1))
                    g = pvT[:, V_NORM[m] + 4 * h:V_NORM[m] + 4 * h + 4].unsqueeze(2).to_broadcast([P, 4, P])
                    nc.vector.tensor_tensor(tg[:, q % 2, :].rearrange("p (k n) -> p k n", k=4),
                                            ps[:, 2 + q, :].rearrange("p (k n) -> p k n", k=4), g,
                                            ALU.mult).then_inc(tg_done, 1)

                def rest(q):
                    t, h = q // 2, q % 2
                    dve.wait_ge(uh_done, l * 16 + (4 * m + q + 1))
                    at = (slice(None), slice(4 * h, 4 * h + 4), slice(t * P, (t + 1) * P))
                    nc.vector.tensor_tensor(uL[at], tg[:, q % 2, :].rearrange("p (k n) -> p k n", k=4),
                                            uH[at].bitcast(F32), ALU.subtract).then_inc(ul_done, 1)

                if m == 0:
                    dve.wait_ge(pvt_done, l + 1)
                gained(0)
                gained(1)
                rest(0)
                gained(2)
                rest(1)
                gained(3)
                rest(2)
                rest(3)

            def residual(l, scale, t0_sem, t0_count, unit, say):
                for q in range(4):
                    t, h = q // 2, q % 2
                    if q == 0:
                        dve.wait_ge(t0_sem, t0_count)
                    if q == 2:
                        dve.wait_ge(wt_used, used(l, unit))
                    s = scale if isinstance(scale, float) else scale[:, t:t + 1]
                    at = xres[:, t, 512 * h:512 * h + 512]
                    nc.vector.scalar_tensor_tensor(at, ps[:, 2 + q, :], s, at, ALU.mult, ALU.add).then_inc(say, 1)

            def hidden(l, f, i):
                for t in range(NT):
                    dve.wait_ge(sil_done, l * (4 * NFC) + i * 2 + (f * 2 * NFC + t + 1))
                    nc.vector.scalar_tensor_tensor(hid[:, t, :], ps[:, t, FC:2 * FC], rs[:, t:t + 1], sil[:, t, :],
                                                   ALU.mult, ALU.mult).then_inc(hid_done, 1)

            def hidden_L(l, f, i):
                dve.wait_ge(hh_done, l * (2 * NFC) + i + (f * NFC + 1))
                nc.vector.tensor_tensor(hTL[:], ps[:, 6, :].rearrange("p (k n) -> p k n", k=2),
                                        hTH[:].bitcast(F32), ALU.subtract).then_inc(hl_done, 1)

            def ffn(l, f):
                base = FFN_BASE[f]
                split_at(l, base + 2)
                split_at(l, base + 3)
                hidden(l, f, 0)
                if f == 0:
                    dve.wait_ge(pth_done, l + 1)
                    nc.vector.tensor_tensor(pTL[:], ps[:, 7, :].rearrange("p (k n) -> p k n", k=2),
                                            pTH[:].bitcast(F32), ALU.subtract).then_inc(ptl_done, 1)
                with dve.Fori(1, NFC) as i:
                    hidden_L(l, f, i - 1)
                    for part in range(3):
                        if part == 2:
                            hidden(l, f, i)
                        u = base + 1 + part
                        split(l, i * 3 + u, u % SLOTS)
                hidden_L(l, f, NFC - 1)
                split_at(l, base + 3 * NFC + 1)
                residual(l, 0.5, acc_t0, l * 5 + (1, 4)[f], base + 3 * NFC - 1, x_ready)

            def two(ap):
                return ap.unsqueeze(1).to_broadcast([P, 2, SEQ])

            def z_evac(l, j):
                dve.wait_ge(wt_used, used(l, U_IN + j))
                src = ps[:, j % 2, :].rearrange("p (i n) -> p i n", i=2)
                i = slice(2 * (j % 2), 2 * (j % 2) + 2)
                if j < 2:
                    dst, other = us[:, i, :], two(rsb[:])
                elif j < 4:
                    dst, other = cy[:, i, :], two(rsb2[:])
                elif j < 6:
                    dst, other = vv[:, i, 2:SEQ + 2], cy[:, i, :]
                else:
                    dve.wait_ge(conv_done, l * 4 + (2 * (j - 6) + 2))
                    dst, other = cy[:, i, :], cy[:, i, :]
                nc.vector.tensor_tensor(dst, src, other, ALU.mult).then_inc(z_out, 1)

            def rotate_in(l, h):
                cs = slice(8 * h, 8 * h + 8)
                co, si = cosT[:, cs, :].rearrange("p b c -> p (b c)"), sinT[:, cs, :].rearrange("p b c -> p (b c)")
                if h == 0:
                    dve.wait_ge(dl_ps, l + 1)
                else:
                    dve.wait_ge(s_done, l * 4 + 2)
                re, im = ps[:, 2 + h, :], ps[:, 4 + h, :]
                for n, (a, b) in enumerate(((re, co), (im, si), (im, co), (re, si))):
                    nc.vector.tensor_tensor(mm[:, n, :], a, b, ALU.mult).then_inc(rot_in, 1)
                dve.wait_ge(rot_in, l * 8 + (4 * h + 2))
                link(l, nc.vector.tensor_tensor(zr, mm[:, 0, :], mm[:, 1, :], ALU.add))

            def scan_and_rotate_out(l, h):
                cs = slice(8 * h, 8 * h + 8)
                co, si = cosT[:, cs, :].rearrange("p b c -> p (b c)"), sinT[:, cs, :].rearrange("p b c -> p (b c)")
                de = decay[:, cs, :].rearrange("p b c -> p (b c)")
                nc.vector.tensor_tensor_scan(zr, de, zr, 0.0, ALU.mult, ALU.add).then_inc(scan_done, 1)
                dve.wait_ge(zi_done, l * 2 + (h + 1))
                nc.vector.tensor_tensor_scan(zi, de, zi, 0.0, ALU.mult, ALU.add).then_inc(scan_done, 1)
                dve.wait_ge(scan_done, l * 4 + (2 * h + 2))
                for n, (a, b) in enumerate(((zr, co), (zi, si), (zi, co), (zr, si))):
                    nc.vector.tensor_tensor(mm[:, n, :], a, b, ALU.mult).then_inc(rot_out, 1)

            def rest_y(l, k, gain):
                src = (cy, zgT)[k]
                for i in range(NCH):
                    dve.wait_ge(yh_done, l * 8 + (4 * k + i + 1))
                    nc.vector.scalar_tensor_tensor(uL[:, i, :], src[:, i, :], pvT[:, gain + i:gain + i + 1],
                                                   uH[:, i, :].bitcast(F32), ALU.mult, ALU.subtract).then_inc(yl_done, 1)

            def mean_y(l, k):
                dve.wait_ge(st_ps, l * 2 + (k + 1))
                nc.vector.tensor_scalar(ms_y[:, k, :], ps[:, 6 * k, 0:NT], 1.0 / CW, (EPS, 4 * EPS)[k],
                                        ALU.mult, ALU.add).then_inc(msy_done, 1)

            def mixer(l):
                split_at(l, U_IN + 2)
                dve.wait_ge(rs_done, l * 4 + 2)
                for t in range(NT):
                    nc.vector.tensor_scalar(diag[:, t, :], ident[:], rs[:, t:t + 1], None, ALU.mult).then_inc(diag_done, 1)
                dve.wait_ge(rsb_ps, l + 1)
                link(l, nc.vector.tensor_copy(rsb[:], ps[:, 7, 0:SEQ]))
                z_evac(l, 0)
                link(l, nc.vector.tensor_tensor(rsb2[:], rsb[:], rsb[:], ALU.mult))
                split_at(l, U_IN + 3)
                z_evac(l, 1)
                dve.wait_ge(z_out, l * 8 + 2)
                for s in range(2, 4):
                    for q in range(4):
                        nc.vector.tensor_copy(u4q[32 * s:32 * s + 32, :, q, :],
                                              usq[32 * q:32 * q + 32, :, :, s]).then_inc(u4d_done, 1)
                split_at(l, U_IN + 4)
                z_evac(l, 2)
                split_at(l, U_IN + 5)
                z_evac(l, 3)
                rotate_in(l, 0)
                split_at(l, U_IN + 6)
                scan_and_rotate_out(l, 0)
                dve.wait_ge(z_out, l * 8 + 4)
                z_evac(l, 4)
                rotate_in(l, 1)
                split_at(l, U_IN + 7)
                z_evac(l, 5)
                scan_and_rotate_out(l, 1)
                split_at(l, U_WOUT_A)
                z_evac(l, 6)
                split_at(l, U_WOUT_A + 1)
                z_evac(l, 7)
                rest_y(l, 0, V_GA)
                mean_y(l, 0)
                split_at(l, U_GLU)
                for h in range(2):
                    at = t1[:, 512 * h:512 * h + 512]
                    dve.wait_ge(ysq_done, l * 2 + (h + 1))
                    link(l, nc.vector.tensor_scalar(at, at, 0.044715, 1.0, ALU.mult, ALU.add))
                    nc.vector.tensor_tensor(at, ps[:, 6 + h, :], at, ALU.mult).then_inc(cub_done, 1)
                for h in range(2):
                    dve.wait_ge(tanh_done, l * 2 + (h + 1))
                    nc.vector.scalar_tensor_tensor(t1[:, 512 * h:512 * h + 512], th[:, 512 * h:512 * h + 512], 1.0,
                                                   ps[:, 6 + h, :], ALU.add, ALU.mult).then_inc(zg_done, 1)
                dve.wait_ge(zg_done, l * 2 + 2)
                for s in range(2, 4):
                    for q in range(4):
                        nc.vector.tensor_scalar(zgq[32 * q:32 * q + 32, :, :, s], t1q[32 * s:32 * s + 32, :, q, :],
                                                0.5, None, ALU.mult).then_inc(zgd_done, 1)
                dve.wait_ge(zgh_done, l + 1)
                nc.vector.tensor_tensor(uL[:, NCH:2 * NCH, :], zgT, uH[:, NCH:2 * NCH, :].bitcast(F32),
                                        ALU.subtract).then_inc(zgl_done, 1)
                split_at(l, U_WOUT_S)
                dve.wait_ge(rsy_done, l * 2 + 1)
                residual(l, rs_y[:, 0, :], acc_t0, l * 5 + 2, U_WOUT_A + 1, xa_done)
                split_at(l, U_WOUT_S + 1)
                for h in range(2):
                    dve.wait_ge(th2_done, l * 4 + (2 * h + 2))
                    at = zgT[:, 2 * h:2 * h + 2, :]
                    nc.vector.scalar_tensor_tensor(at, thv[:, 2 * h:2 * h + 2, :], 1.0, at,
                                                   ALU.add, ALU.mult).then_inc(yy_done, 1)
                rest_y(l, 1, V_GS)
                mean_y(l, 1)
                split_at(l, U_FFN2)
                split_at(l, U_FFN2 + 1)
                dve.wait_ge(rsy_done, l * 2 + 2)
                dve.wait_ge(xa_done, l * 4 + 4)
                residual(l, rs_y[:, 1, :], acc_t0, l * 5 + 3, U_WOUT_S + 1, x_ready)

            def embedding(l):
                norm(l, 3)
                split_at(l, U_GATE + 1)
                split_at(l, U_GATE + 2)
                split_at(l, U_GATE + 3)
                for q in range(4):
                    at = bufB[:, (q % 2) * 512:(q % 2) * 512 + 512]
                    t, h = q // 2, q % 2
                    pq = pp[:, t, 512 * h:512 * h + 512]
                    dve.wait_ge(pp_done, l * 4 + (q + 1))
                    dve.wait_ge(gate_done, l * 4 + (q + 1))
                    nc.vector.scalar_tensor_tensor(pq, at, 1.0, pq, ALU.add, ALU.mult).then_inc(gx_done, 1)
                    dve.wait_ge(gx_done, l * 4 + (q + 1))
                    xq = xres[:, t, 512 * h:512 * h + 512]
                    nc.vector.tensor_tensor(xq, xq, pq, ALU.add).then_inc(x_ready, 1)

            with dve.Fori(0, DEPTH) as l:
                split_at(l, 0)
                norm(l, 0)
                split_at(l, 1)
                ffn(l, 0)
                norm(l, 1)
                mixer(l)
                norm(l, 2)
                ffn(l, 1)
                embedding(l)
            assert links[0] == DVE_LINKS, links
            dve.wait_ge(rs_done, 4 * DEPTH + 1)
            dve.wait_ge(fin_ld, 16)
            for t in range(NT):
                nc.vector.scalar_tensor_tensor(xres[:, t, :], xres[:, t, :], rs[:, t:t + 1], regT[:, 0:D],
                                               ALU.mult, ALU.mult).then_inc(fin_done, 1)

        @block.gpsimd
        def _(pool):
            g = nc.gpsimd
            g.memset(ident[:], 0.0).then_inc(consts, 1)
            g.memset(ones[:], 1.0).then_inc(consts, 1)
            g.memset(pvec[:], 0.0).then_inc(consts, 1)
            g.memset(mhalf[:], -0.5).then_inc(consts, 1)
            g.memset(mone[:], -1.0).then_inc(consts, 1)
            for t in range(NCH):
                last = g.memset(vv[:, t, 0:2], 0.0)
            last.then_inc(consts, 1)
            g.memset(taps[:], 0.0).then_inc(consts, 1)
            pool.wait_ge(consts, 7)
            g.affine_select(out=ident[:], in_=ident[:], compare_op=ALU.not_equal, fill=1.0, base=0,
                            pattern=[[-1, P]], channel_multiplier=1).then_inc(consts, 1)
            g.memset(Gr[:], 0.0).then_inc(consts, 1)
            g.memset(Gi[:], 0.0).then_inc(consts, 1)
            pool.wait_ge(consts, 10)
            links = [0]

            def inv_rms(l, m):
                four = 4.0 if m == 3 else 1.0
                pool.wait_ge(ssq_done, l * 8 + (2 * m + 2))
                pool.sem_inc(passed, 1)
                link(l, g.tensor_scalar(ms[:], ssq[:], four / D, four * EPS, ALU.mult, ALU.add))
                g.tensor_tensor(rs[:], ms[:], mhalf[:, 0:NT], ALU.pow).then_inc(rs_done, 1)

            def link(l, ins):
                links[0] += 1
                ins.then_inc(pool_link, 1)
                pool.wait_ge(pool_link, links[0])

            def setup(l):
                def tt(o, a, b, op):
                    link(l, g.tensor_tensor(o, a, b, op))

                def ts(o, a, s1, s2, op1=ALU.mult, op2=ALU.add):
                    link(l, g.tensor_scalar(o, a, s1, s2, op1, op2))

                v = lambda n: prm[:, n, :]
                (DT, X, N_, R, Q, TMP, EM, E_, PH, SI, CO, CM, NR, NI, LR, MAG, DEN, FR, FI, A2R, A2I, A3R, A3I,
                 A4R, A4I, NLI, NA2I, NA3I, NA4I, SHI, CHI, W) = range(32)

                def exp_parts(src):
                    ts(v(X), src, -87.0, 88.0, ALU.max, ALU.min)
                    ts(v(N_), v(X), LOG2E, ROUND)
                    ts(v(N_), v(N_), -ROUND, 1.0, ALU.add, ALU.mult)
                    ts(v(TMP), v(N_), -LN2_HI, 0.0)
                    tt(v(R), v(X), v(TMP), ALU.add)
                    ts(v(TMP), v(N_), -LN2_LO, 0.0)
                    tt(v(R), v(R), v(TMP), ALU.add)
                    ts(v(Q), v(R), 1 / 5040, 1 / 720)
                    for c in (1 / 120, 1 / 24, 1 / 6, 1 / 2, 1.0):
                        tt(v(Q), v(Q), v(R), ALU.mult)
                        ts(v(Q), v(Q), c, 1.0, ALU.add, ALU.mult)
                    tt(v(Q), v(Q), v(R), ALU.mult)
                    ts(prmi[:], v(N_), 127.0, 8388608.0, ALU.add, ALU.mult)
                    pow2 = prmi[:].bitcast(F32)
                    tt(v(Q), v(Q), pow2, ALU.mult)
                    ts(v(EM), pow2, -1.0, 1.0, ALU.add, ALU.mult)
                    tt(v(EM), v(EM), v(Q), ALU.add)
                    tt(v(E_), pow2, v(Q), ALU.add)

                ar, ai = pvT[:, V_AR:V_AR + NB], pvT[:, V_AI:V_AI + NB]
                exp_parts(pvT[:, V_LDT:V_LDT + NB])
                ts(v(TMP), pvT[:, V_LDT:V_LDT + NB], -87.33, 1.0, ALU.is_ge, ALU.mult)
                tt(v(DT), v(E_), v(TMP), ALU.mult)
                tt(v(TMP), ar, v(DT), ALU.mult)
                exp_parts(v(TMP))
                ts(v(MAG), v(EM), 1.0, 1.0, ALU.add, ALU.mult)
                tt(v(PH), ai, v(DT), ALU.mult)
                ts(v(N_), v(PH), 1 / (2 * math.pi), ROUND)
                ts(v(N_), v(N_), -ROUND, 1.0, ALU.add, ALU.mult)
                for c in (TWO_PI_1, TWO_PI_2, TWO_PI_3):
                    ts(v(TMP), v(N_), -c, 0.0)
                    tt(v(PH), v(PH), v(TMP), ALU.add)
                ts(v(PH), v(PH), 0.5, 0.0)
                tt(v(W), v(PH), v(PH), ALU.mult)
                for o, first in ((SHI, 13), (CHI, 14)):
                    ts(v(o), v(W), (-1) ** (first // 2) / math.factorial(first),
                       (-1) ** (first // 2 - 1) / math.factorial(first - 2))
                    for k in range(first - 4, -1, -2):
                        tt(v(o), v(o), v(W), ALU.mult)
                        ts(v(o), v(o), (-1) ** (k // 2) / math.factorial(k), 1.0, ALU.add, ALU.mult)
                tt(v(SHI), v(SHI), v(PH), ALU.mult)
                tt(v(SI), v(SHI), v(CHI), ALU.mult)
                ts(v(SI), v(SI), 2.0, 0.0)
                tt(v(CM), v(SHI), v(SHI), ALU.mult)
                ts(v(CM), v(CM), -2.0, 0.0)
                ts(v(CO), v(CM), 1.0, 1.0, ALU.add, ALU.mult)
                tt(v(NR), v(EM), v(CO), ALU.mult)
                tt(v(NR), v(NR), v(CM), ALU.add)
                tt(v(NI), v(MAG), v(SI), ALU.mult)
                ts(v(LR), v(NR), 1.0, 1.0, ALU.add, ALU.mult)
                tt(v(DEN), ar, ar, ALU.mult)
                tt(v(TMP), ai, ai, ALU.mult)
                tt(v(DEN), v(DEN), v(TMP), ALU.add)
                tt(v(DEN), v(DEN), mone[:], ALU.pow)
                tt(v(FR), v(NR), ar, ALU.mult)
                tt(v(TMP), v(NI), ai, ALU.mult)
                tt(v(FR), v(FR), v(TMP), ALU.add)
                tt(v(FR), v(FR), v(DEN), ALU.mult)
                tt(v(FI), v(NI), ar, ALU.mult)
                tt(v(TMP), v(NR), ai, ALU.mult)
                tt(v(FI), v(FI), v(TMP), ALU.subtract)
                tt(v(FI), v(FI), v(DEN), ALU.mult)

                def cmul(o_r, o_i, a_r, a_i, b_r, b_i, p1, p2):
                    tt(p1, a_r, b_r, ALU.mult)
                    tt(p2, a_i, b_i, ALU.mult)
                    for o, sl in o_r:
                        tt(o, p1[sl], p2[sl], ALU.subtract)
                    tt(p1, a_r, b_i, ALU.mult)
                    tt(p2, a_i, b_r, ALU.mult)
                    for o, sl in o_i:
                        tt(o, p1[sl], p2[sl], ALU.add)

                whole = slice(None)
                for (o_r, o_i), (a_r, a_i), (b_r, b_i) in (((A2R, A2I), (LR, NI), (LR, NI)), ((A3R, A3I), (A2R, A2I), (LR, NI)),
                                                           ((A4R, A4I), (A2R, A2I), (A2R, A2I))):
                    cmul([(v(o_r), whole)], [(v(o_i), whole)], v(a_r), v(a_i), v(b_r), v(b_i), v(TMP), v(W))
                powers = [None, (LR, NI), (A2R, A2I), (A3R, A3I), (A4R, A4I)]

                def tab(c, w=1):
                    return cosT[:, :, c:c + w], sinT[:, :, c:c + w]

                c0, s0 = cosT[:, :, 0], sinT[:, :, 0]
                cmul([(v(Q), whole)], [(v(R), whole)], v(CO), v(SI), v(CO), v(SI), v(TMP), v(W))
                cmul([(c0, whole)], [(s0, whole)], v(Q), v(R), v(Q), v(R), v(TMP), v(W))
                w = 1
                while w < NCK:
                    by = [a.to_broadcast([P, NB, w]) for a in tab(w - 1)]
                    o = tab(w, w)
                    src = tab(0, w)
                    cmul([(o[0], whole)], [(o[1], whole)], src[0], src[1], by[0], by[1], pa[:, :, 0:w], pb[:, :, 0:w])
                    w *= 2
                tt(v(W), v(MAG), v(MAG), ALU.mult)
                tt(v(W), v(W), v(W), ALU.mult)
                g.tensor_copy(decay[:, :, 1:NCK], v(W).unsqueeze(2).to_broadcast([P, NB, NCK - 1])).then_inc(pool_link, 1)
                links[0] += 1
                g.memset(decay[:, :, 0:1], 0.0).then_inc(pool_link, 1)
                links[0] += 1

                pool.wait_ge(bc_ld, (l + 1) * (16 * NBC))
                pool.sem_inc(passed, 1)
                g.memset(regE[:], 0.0).then_inc(pool_link, 1)
                links[0] += 1
                pool.wait_ge(pool_link, links[0])

                def over_h(n):
                    return v(n).unsqueeze(2).to_broadcast([P, NB, GRP])

                def halves(buf, k):
                    return [(buf[64 * q:64 * q + 64, :, k, GRP * q:GRP * q + GRP], slice(64 * q, 64 * q + 64)) for q in range(2)]

                pah, pbh = pa[:, :, 0:GRP], pb[:, :, 0:GRP]
                cmul([(bbr, whole)], [(bbi, whole)], over_h(FR), over_h(FI), br, bi, pah, pbh)
                for o, src in ((Er, bbr), (Ei, bbi)):
                    for part, sl in halves(o, T - 1):
                        link(l, g.tensor_copy(part, src[sl]))
                for k in range(1, T):
                    n_r, n_i = powers[k]
                    cmul(halves(Er, T - 1 - k), halves(Ei, T - 1 - k), over_h(n_r), over_h(n_i), bbr, bbi, pah, pbh)
                pool.wait_ge(ct_done, l * 4 + 4)
                pool.sem_inc(passed, 1)
                for o, src in ((Gr, cr), (Gi, nci)):
                    for part, sl in halves(o, 0):
                        link(l, g.tensor_copy(part, src[sl]))
                for k in range(1, T + 1):
                    n_r, n_i = powers[k]
                    ts(v(W), v(n_i), -1.0, 0.0)
                    cmul(halves(Gr, k), halves(Gi, k), cr, nci, over_h(n_r), over_h(W), pah, pbh)
                pool.wait_ge(pt_ps, l + 1)
                g.tensor_tensor(dtmp[96:128], ident[96:128, 96:128].unsqueeze(1).to_broadcast([32, NB, 32]),
                                pvT[96:128, V_D:V_D + NB].unsqueeze(2).to_broadcast([32, NB, 32]),
                                ALU.mult).then_inc(ssm_ready, 1)
                pool.wait_ge(ssm_ready, l + 1)
                pool.sem_inc(passed, 1)

            def mixer(l):
                pool.wait_ge(rs_done, l * 4 + 2)
                pool.wait_ge(kc_done, l + 1)
                g.tensor_tensor(kc[96:128], kc[96:128], dtmp[96:128], ALU.add).then_inc(kc_full, 1)
                pool.wait_ge(kc_full, l + 1)

                def state_half(h):
                    pool.wait_ge(rot_in, l * 8 + (4 * h + 4))
                    g.tensor_tensor(zi, mm[:, 2, :], mm[:, 3, :], ALU.subtract).then_inc(zi_done, 1)
                    pool.wait_ge(rot_out, l * 8 + (4 * h + 4))
                    at = slice(8 * h, 8 * h + 8)
                    g.tensor_tensor(Sr[:, at, :].rearrange("p b c -> p (b c)"), mm[:, 0, :], mm[:, 1, :],
                                    ALU.subtract).then_inc(s_done, 1)
                    g.tensor_tensor(Si[:, at, :].rearrange("p b c -> p (b c)"), mm[:, 2, :], mm[:, 3, :],
                                    ALU.add).then_inc(s_done, 1)

                def conv(i):
                    cw = lambda j: pvT[:, V_CW + NCH * j + i:V_CW + NCH * j + i + 1]
                    o = cy[:, i, :]
                    link(l, g.tensor_scalar(o, vv[:, i, 2:SEQ + 2], cw(2), pvT[:, V_CB + i:V_CB + i + 1], ALU.mult, ALU.add))
                    for j in (1, 0):
                        link(l, g.tensor_scalar(ctmp[:], vv[:, i, j:SEQ + j], cw(j), 0.0, ALU.mult, ALU.add))
                        link(l, g.tensor_tensor(o, o, ctmp[:], ALU.add))
                    g.tensor_tensor(o, o, rsb[:], ALU.mult).then_inc(conv_done, 1)

                state_half(0)
                state_half(1)
                pool.wait_ge(z_out, l * 8 + 6)
                pool.sem_inc(passed, 1)
                for i in range(NCH):
                    conv(i)
                for k in range(2):
                    pool.wait_ge(msy_done, l * 2 + (k + 1))
                    g.tensor_tensor(rs_y[:, k, :], ms_y[:, k, :], mhalf[:, 0:NT], ALU.pow).then_inc(rsy_done, 1)

            with pool.Fori(0, DEPTH) as l:
                pool.sem_clear(pool_link)
                pool.wait_ge(vec_ld, (l + 1) * (16 * NPV))
                pool.sem_inc(passed, 1)
                g.tensor_copy(pvec[V_LDT:V_LDT + NB, :].rearrange("b (g p) -> b g p", g=2),
                              ldt[V_LDT:V_LDT + NB, :].unsqueeze(2).to_broadcast([NB, 2, ST])).then_inc(pv_full, 1)
                pool.wait_ge(pv_full, l + 1)
                inv_rms(l, 0)
                pool.wait_ge(pvt_done, l + 1)
                pool.sem_inc(passed, 1)
                setup(l)
                inv_rms(l, 1)
                mixer(l)
                inv_rms(l, 2)
                inv_rms(l, 3)
                pool.wait_ge(rs_done, l * 4 + 4)
                pool.sem_inc(passed, 1)
            links[0] = 0
            pool.sem_clear(pool_link)
            inv_rms(DEPTH, 0)

        @block.tensor
        def _(pe):
            mul = nc.tensor.matmul
            pe.sem_inc(wt_used, SLOTS)
            pe.wait_ge(consts, 10)

            def mm3(o, sH, sL, vH, vL, start, stop):
                mul(o, sH, vH, start=start, stop=False)
                mul(o, sH, vL, start=False, stop=False)
                return mul(o, sL, vH, start=False, stop=stop)

            def take(l, n):
                pe.wait_ge(wl_done, l * UNITS + n + (1 + SLOTS))

            def norm(l, m):
                for q in range(4):
                    t, h = q // 2, q % 2
                    pe.wait_ge(x_ready, l * 16 + (16 + 4 * m + q + 1))
                    for k in range(4):
                        last = nc.tensor.transpose(ps[:, 2 + q, k * P:(k + 1) * P],
                                                   xres[:, t, (4 * h + k) * P:(4 * h + k + 1) * P], ident[:])
                    last.then_inc(xt_ps, 1)

            def gate_up(l, f, i, n, slot, part):
                take(l, n)
                for t in range(NT):
                    if isinstance(i, int) and i == 0:
                        pe.wait_ge(ul_done, l * 16 + (8 * f + 2 * t + part + 1))
                    for k in range(4):
                        at = (slice(None), 4 * part + k, slice(t * P, (t + 1) * P))
                        w = slice(512 * k, 512 * k + 512)
                        last = mm3(ps[:, t, :], uH[at], uL[at], wH[:, slot, w], wL[:, slot, w],
                                   part == 0 and k == 0, part == 1 and k == 3)
                    if t == 1:
                        last.then_inc(wt_used, 1)
                    elif part == 1:
                        last.then_inc(gu_t0, 1)

            def rows2(l, n, slot, sH, sL, k0, banks, first, end, say_t0):
                take(l, n)
                for t in range(NT):
                    for k in range(2):
                        at = (slice(None), k0 + k, slice(t * P, (t + 1) * P))
                        for h in range(2):
                            w = slice(D * k + 512 * h, D * k + 512 * h + 512)
                            last = mm3(ps[:, banks[2 * t + h], :], sH[at], sL[at], wH[:, slot, w], wL[:, slot, w],
                                       first and k == 0, end and k == 1)
                    if t == 1:
                        last.then_inc(wt_used, 1)
                    elif say_t0:
                        last.then_inc(acc_t0, 1)

            ACC = (2, 3, 4, 5)

            def down(l, f, i, n, slot, first=False, end=False):
                pe.wait_ge(hl_done, l * (2 * NFC) + i + (f * NFC + 1))
                rows2(l, n, slot, hTH, hTL, 0, ACC, first, end, end)

            def turn_hidden(l, f, i):
                pe.wait_ge(hid_done, l * (4 * NFC) + i * 2 + (f * 2 * NFC + 2))
                for k in range(2):
                    for t in range(NT):
                        last = nc.tensor.transpose(ps[:, 6, k * SEQ + t * P:k * SEQ + (t + 1) * P],
                                                   hid[:, t, k * P:(k + 1) * P], ident[:])
                last.then_inc(ht_ps, 1)

            def step(l, f, i, first=False):
                base = FFN_BASE[f]
                for part in range(2):
                    gate_up(l, f, i, i * 3 + (base - 1 + part), (base - 1 + part) % SLOTS, part)
                down(l, f, i - 1, i * 3 + (base + 1), (base + 1) % SLOTS, first=first)
                turn_hidden(l, f, i)

            def turn_params(l, which):
                if which < 2:
                    if which == 0:
                        pe.wait_ge(pvt_done, l + 1)
                        pe.wait_ge(bc_ld, (l + 1) * (16 * NBC))
                    else:
                        pe.wait_ge(ct_done, l * 4 + 2)
                    for q in range(4):
                        last = nc.tensor.transpose(ps[:, 7, q * P:(q + 1) * P],
                                                   cnat[:, which, q, :, :].rearrange("p d c -> p (d c)"), ident[:])
                    last.then_inc(ct_ps, 1)
                else:
                    pe.wait_ge(ct_done, l * 4 + 4)
                    for k in range(2):
                        for t in range(NT):
                            last = nc.tensor.transpose(ps[:, 7, k * SEQ + t * P:k * SEQ + (t + 1) * P],
                                                       pnat[:, t, k * P:(k + 1) * P], ident[:])
                    last.then_inc(pt_ps, 1)

            def ffn(l, f):
                base = FFN_BASE[f]
                for part in range(2):
                    gate_up(l, f, 0, base + part, (base + part) % SLOTS, part)
                if f == 0:
                    turn_params(l, 0)
                turn_hidden(l, f, 0)
                if f == 0:
                    turn_params(l, 1)
                    turn_params(l, 2)
                step(l, f, 1, first=True)
                with pe.Fori(2, NFC) as i:
                    step(l, f, i)
                n = base + 3 * NFC - 1
                down(l, f, NFC - 1, n, n % SLOTS, end=True)

            def w_in_unit(l, j):
                n = U_IN + j
                take(l, n)
                if j == 0:
                    pe.wait_ge(ul_done, l * 16 + 8)
                if j >= 2:
                    pe.wait_ge(z_out, l * 8 + (j - 1))
                w = wH[:, n % SLOTS, :].rearrange("p (k c) -> p k c", k=KD)
                r = wL[:, n % SLOTS, :].rearrange("p (k c) -> p k c", k=KD)
                for i in range(2):
                    for k in range(KD):
                        c = slice(i * P, (i + 1) * P)
                        last = mm3(ps[:, j % 2, i * SEQ:(i + 1) * SEQ], w[:, k, c], r[:, k, c], uH[:, k, :], uL[:, k, :],
                                   k == 0, k == KD - 1)
                last.then_inc(wt_used, 1)

            def turn_E(l, r):
                src = (Er, Ei)[r]
                for b in range(4):
                    if r == 1:
                        pe.wait_ge(et_done, l * 8 + (b + 1))
                    for j in range(4):
                        last = nc.tensor.transpose(ps[:, 2 + b, j * P:(j + 1) * P],
                                                   src[:, 4 * b + j, :, :].rearrange("p s c -> p (s c)"), ident[:])
                    last.then_inc(et_ps, 1)

            def stats(l, k):
                pe.wait_ge(sq_done, l * 2 + (k + 1))
                for t in range(NT):
                    for i in range(NCH):
                        last = mul(ps[:, 6 * k, t:t + 1], sqy[:, i, t * P:(t + 1) * P], ones[:, 0:1],
                                   start=(i == 0), stop=(i == NCH - 1))
                last.then_inc(st_ps, 1)

            def mixer(l):
                w_in_unit(l, 0)
                pe.wait_ge(diag_done, l * 2 + 2)
                pe.wait_ge(ptl_done, l + 2)
                for t in range(NT):
                    last = mul(ps[:, 7, t * P:(t + 1) * P], ones[:], diag[:, t, :], start=True, stop=True)
                last.then_inc(rsb_ps, 1)
                pe.wait_ge(ssm_ready, l + 1)
                turn_E(l, 0)
                w_in_unit(l, 1)
                turn_E(l, 1)
                for b in range(NB):
                    o = ps[:, 6, 32 * b:32 * b + 32]
                    mul(o, Er[:, b, :, :].rearrange("p s c -> p (s c)"), Gr[:, b, 0, :], start=True, stop=False)
                    last = mul(o, Ei[:, b, :, :].rearrange("p s c -> p (s c)"), Gi[:, b, 0, :], start=False, stop=True)
                last.then_inc(kc_ps, 1)
                w_in_unit(l, 2)
                pe.wait_ge(u4a_done, l * 8 + 8)
                pe.wait_ge(u4d_done, l * 8 + 8)
                pe.wait_ge(et_done, l * 8 + 8)
                for b in range(NB):
                    c = slice(NCK * (b % 8), NCK * (b % 8) + NCK)
                    mul(ps[:, 2 + b // 8, c], ETr[:, b, :], u4[:, b, :], start=True, stop=True)
                    last = mul(ps[:, 4 + b // 8, c], ETi[:, b, :], u4[:, b, :], start=True, stop=True)
                last.then_inc(dl_ps, 1)
                for j in range(3, 8):
                    w_in_unit(l, j)
                pe.wait_ge(taps_done, l * 10 + 10)
                pe.wait_ge(s_done, l * 4 + 4)
                for b in range(NB):
                    c = NCK * (b % 8)
                    bank = 6 + b // 8
                    gr = Gr[:, b, 1:T + 1, :].rearrange("p k c -> p (k c)")
                    gi = Gi[:, b, 1:T + 1, :].rearrange("p k c -> p (k c)")
                    mul(ps[:, bank, c:c + NCK], taps[:, b, :], u4[:, b, :], start=True, stop=False)
                    mul(ps[:, bank, c + 1:c + NCK], gr, Sr[:, b, 0:NCK - 1], start=False, stop=False)
                    last = mul(ps[:, bank, c + 1:c + NCK], gi, Si[:, b, 0:NCK - 1], start=False, stop=True)
                    if b % 8 == 7:
                        last.then_inc(y_ps, 1)
                pe.wait_ge(z_out, l * 8 + 8)
                stats(l, 0)
                pe.wait_ge(yl_done, l * 8 + 4)
                for j in range(2):
                    n = U_WOUT_A + j
                    rows2(l, n, n % SLOTS, uH, uL, 2 * j, ACC, j == 0, j == 1, j == 1)
                take(l, U_GLU)
                pe.wait_ge(zgl_done, l + 1)
                pe.wait_ge(msy_done, l * 2 + 1)
                w = wH[:, U_GLU % SLOTS, :].rearrange("p (k c) -> p k c", k=NCH)
                r = wL[:, U_GLU % SLOTS, :].rearrange("p (k c) -> p k c", k=NCH)
                for i in range(NCH):
                    for k in range(NCH):
                        c = slice(i * P, (i + 1) * P)
                        last = mm3(ps[:, i // 2, (i % 2) * SEQ:(i % 2 + 1) * SEQ], w[:, k, c], r[:, k, c],
                                   uH[:, NCH + k, :], uL[:, NCH + k, :], k == 0, k == NCH - 1)
                    if i == 1:
                        last.then_inc(glu_h0, 1)
                last.then_inc(wt_used, 1)
                pe.wait_ge(xa_done, l * 4 + 4)
                for j in range(2):
                    n = U_WOUT_S + j
                    if j == 0:
                        pe.wait_ge(yl_done, l * 8 + 8)
                    rows2(l, n, n % SLOTS, uH, uL, 2 * j, ACC, j == 0, j == 1, j == 1)
                    if j == 0:
                        stats(l, 1)

            def embedding(l):
                rows2(l, U_PROJ, U_PROJ % SLOTS, pTH, pTL, 0, (0, 1, 6, 7), True, True, False)
                norm(l, 3)
                for j in range(4):
                    n = U_GATE + j
                    if j == 0:
                        pe.wait_ge(ul_done, l * 16 + 16)
                        pe.wait_ge(pp_done, l * 4 + 4)
                    rows2(l, n, n % SLOTS, uH, uL, 2 * j, ACC, j == 0, j == 3, j == 3)

            with pe.Fori(0, DEPTH) as l:
                pe.wait_ge(pv_full, l + 1)
                nc.tensor.transpose(ps[:, 7, 0:P], pvec[:], ident[:]).then_inc(pvt_ps, 1)
                norm(l, 0)
                ffn(l, 0)
                norm(l, 1)
                mixer(l)
                norm(l, 2)
                ffn(l, 1)
                embedding(l)


_INS = ["x", "p", "ffn1_norm", "ffn1_w_gate", "ffn1_w_up", "ffn1_w_down", "mix_norm", "w_in", "conv_w", "conv_b",
        "ssm_A_re", "ssm_A_im", "ssm_B_re", "ssm_B_im", "ssm_C_re", "ssm_C_im", "ssm_D", "ssm_log_dt", "glu_w",
        "glu_b", "conv_out_norm", "ssm_out_norm", "w_out", "ffn2_norm", "ffn2_w_gate", "ffn2_w_up", "ffn2_w_down",
        "ple_norm", "ple_w_gate", "ple_w_proj", "final_norm"]


def kernel(**inputs):
    import numpy as _np
    import concourse.bacc as _bacc
    from concourse import mybir as _mybir
    from concourse.bass_utils import run_bass_kernel_spmd as _run

    nc = _bacc.Bacc("TRN2", target_bir_lowering=False, num_devices=1)
    arrays, args = {}, []
    for name in _INS:
        a = _np.ascontiguousarray(inputs[name])
        arrays[f"in_{name}_dram"] = a
        args.append(nc.dram_tensor(f"in_{name}_dram", a.shape, _mybir.dt.from_np(a.dtype), kind="ExternalInput").ap())
    args.append(nc.dram_tensor("out_0_dram", (1, SEQ, D), F32, kind="ExternalOutput").ap())
    trunk(nc, *args)
    r = _run(nc, [arrays], core_ids=[0])
    return r.results[0]["out_0_dram"]
```

```python
import math
from contextlib import ExitStack

import concourse.bass as bass
from concourse import mybir

F32 = mybir.dt.float32
F32R = mybir.dt.float32r
I32 = mybir.dt.int32
ALU = mybir.AluOpType
ACT = mybir.ActivationFunctionType

P = 128
D = 1024
SEQ = 256
DEPTH = 2
NT = SEQ // P
KD = D // P
CW = D // 2
NCH = CW // P
FF = 2816
FC = 256
NFC = FF // FC
PLE = 256
EPS = 1e-6
UNIT = 2048
SLOTS = 3

T = 4
NCK = SEQ // T
NB = 16
GRP = 16
ST = 64

U_FFN1 = 0
U_IN = U_FFN1 + 3 * NFC
U_WOUT_A0 = U_IN + 8
U_GLU = U_WOUT_A0 + 1
U_WOUT_A1 = U_GLU + 1
U_WOUT_S = U_WOUT_A1 + 1
U_FFN2 = U_WOUT_S + 2
U_PROJ = U_FFN2 + 3 * NFC
U_GATE = U_PROJ + 1
UNITS = U_GATE + 4
assert UNITS % SLOTS == 0 and UNITS == 84
IN_COLS = [1536, 1792, 512, 768, 1024, 1280, 0, 256]

V_NORM = [0, 8, 16, 24]
V_CW, V_CB, V_GB, V_GA, V_GS = 32, 44, 48, 52, 56
V_AR, V_AI, V_LDT, V_D = 60, 76, 96, 112

LOG2E = 1.4426950408889634
LN2_HI, LN2_LO = 0.693359375, -2.12194440e-4
ROUND = 12582912.0
TWO_PI_1 = 6.28125
TWO_PI_2 = 0.0019350051879882812
TWO_PI_3 = 2 * math.pi - TWO_PI_1 - TWO_PI_2
GELU_C = math.sqrt(2 / math.pi)

ZA = 6
DVE_LINKS = 12
NPV = 12
NBC = 7
ACC = (2, 3, 4, 5)
SIDE_BANKS = (0, 1, 6, 7)


def trunk(nc, x, p, ffn1_norm, ffn1_w_gate, ffn1_w_up, ffn1_w_down, mix_norm, w_in, conv_w, conv_b,
          ssm_A_re, ssm_A_im, ssm_B_re, ssm_B_im, ssm_C_re, ssm_C_im, ssm_D, ssm_log_dt, glu_w, glu_b,
          conv_out_norm, ssm_out_norm, w_out, ffn2_norm, ffn2_w_gate, ffn2_w_up, ffn2_w_down,
          ple_norm, ple_w_gate, ple_w_proj, final_norm, out):
    with ExitStack() as ctx:
        def sb(name, shape, dt=F32):
            return ctx.enter_context(nc.sbuf_tensor(name, shape, dt))

        def sem(name):
            return ctx.enter_context(nc.semaphore(name))

        raw = sb("raw", [P, SLOTS, UNIT])
        wH = sb("wH", [P, SLOTS, UNIT], F32R)
        wL = sb("wL", [P, SLOTS, UNIT], F32R)
        xres = sb("xres", [P, NT, D])
        uH = sb("uH", [P, KD, SEQ], F32R)
        uL = sb("uL", [P, KD, SEQ], F32R)
        tg = sb("tg", [P, 2, 512])
        hTH = sb("hTH", [P, 2, SEQ], F32R)
        hTL = sb("hTL", [P, 2, SEQ], F32R)
        pTH = sb("pTH", [P, 2, SEQ], F32R)
        pTL = sb("pTL", [P, 2, SEQ], F32R)
        pvec = sb("pvec", [P, P])
        pvec0 = sb("pvec0", [P, P])
        pvT = sb("pvT", [P, P])
        ldt = sb("ldt", [P, 2])
        hgb = sb("hgb", [P, NCH])
        pnat = sb("pnat", [P, NT, PLE])
        ident = sb("ident", [P, P])
        ones = sb("ones", [P, P])
        rsb = sb("rsb", [P, SEQ])
        rsb2 = sb("rsb2", [P, SEQ])
        ssq = sb("ssq", [P, NT])
        ms = sb("ms", [P, NT])
        rs = sb("rs", [P, NT])
        ms_y = sb("ms_y", [P, 2, NT])
        rs_y = sb("rs_y", [P, 2, NT])
        mhalf = sb("mhalf", [P, NB])
        mone = sb("mone", [P, NB])
        prm = sb("prm", [P, 28, NB])
        prmi = sb("prmi", [P, NB], I32)
        bufB = sb("bufB", [P, 1024])
        sil = bufB[:, 0:512].rearrange("p (t c) -> p t c", t=NT)
        hid = bufB[:, 512:1024].rearrange("p (t c) -> p t c", t=NT)
        u4 = bufB[:, :].rearrange("p (b c) -> p b c", b=NB)
        bufA = sb("bufA", [P, 2048])
        pp = bufA[:, :].rearrange("p (t n) -> p t n", t=NT)
        us = bufA[:, 0:1024].rearrange("p (i n) -> p i n", i=NCH)
        sqy = us
        cy = bufA[:, 1024:2048].rearrange("p (i n) -> p i n", i=NCH)
        vv = sb("vv", [P, NCH, SEQ + 2])
        ctmp = sb("ctmp", [P, SEQ])
        diag = ctmp[:].rearrange("p (t n) -> p t n", t=NT)
        Gr = sb("Gr", [P, NB, T + 1, 32])
        Gi = sb("Gi", [P, NB, T + 1, 32])
        taps = sb("taps", [P, NB, P])
        kc = sb("kc", [P, NB, 32])
        dtmp = pnat[:].rearrange("p t d -> p (t d)").rearrange("p (b c) -> p b c", b=NB)
        cosT = sb("cosT", [P, NB, NCK])
        sinT = sb("sinT", [P, NB, NCK])
        decay = sb("decay", [P, NB, NCK])
        regE = sb("regE", [P, 4096])
        Er = regE[:, 0:2048].rearrange("p (b s c) -> p b s c", b=NB, s=T)
        Ei = regE[:, 2048:4096].rearrange("p (b s c) -> p b s c", b=NB, s=T)
        Sr = regE[:, 0:1024].rearrange("p (b c) -> p b c", b=NB)
        Si = regE[:, 1024:2048].rearrange("p (b c) -> p b c", b=NB)
        zr, zi = regE[:, 2048:2560], regE[:, 2560:3072]
        t1 = regE[:, 3072:4096]
        regT = sb("regT", [P, 4096])
        ETr = regT[:, 0:2048].rearrange("p (b c) -> p b c", b=NB)
        ETi = regT[:, 2048:4096].rearrange("p (b c) -> p b c", b=NB)
        mm = regT[:, 0:2048].rearrange("p (n c) -> p n c", n=4)
        th = regT[:, 2048:3072]
        zgT = regT[:, 3072:4096].rearrange("p (i n) -> p i n", i=NCH)
        cnat = regT[:, 0:1024].rearrange("p (r q d c) -> p r q d c", r=2, q=4, d=2)
        br = regT[:, 1024:1280].rearrange("p (b h) -> p b h", b=NB)
        bi = regT[:, 1280:1536].rearrange("p (b h) -> p b h", b=NB)
        cr = regT[:, 1536:1792].rearrange("p (b h) -> p b h", b=NB)
        nci = regT[:, 1792:2048].rearrange("p (b h) -> p b h", b=NB)
        bbr = regT[:, 2048:2304].rearrange("p (b h) -> p b h", b=NB)
        bbi = regT[:, 2304:2560].rearrange("p (b h) -> p b h", b=NB)
        pa = regT[:, 2560:3072].rearrange("p (b h) -> p b h", b=NB)
        pb = regT[:, 3072:3584].rearrange("p (b h) -> p b h", b=NB)
        ps = ctx.enter_context(nc.psum_tensor("ps", [P, 8, 512], F32))

        usq = us.rearrange("p i (c s) -> p i c s", s=T)
        u4q = bufB[:, :].rearrange("p (i q c) -> p i q c", i=NCH, q=4)
        t1q = t1.rearrange("p (i q c) -> p i q c", i=NCH, q=4)
        zgq = zgT.rearrange("p i (c s) -> p i c s", s=T)
        thv = th.rearrange("p (i n) -> p i n", i=NCH)

        ld = [sem(f"ld{s}") for s in range(SLOTS)]
        wh_done, wl_half, wl_done, wt_used = sem("wh_done"), sem("wl_half"), sem("wl_done"), sem("wt_used")
        x_ld = [sem(f"x_ld{t}") for t in range(NT)]
        vec0_ld, vec_ld, bc_ld, fin_ld, stored = (sem(n) for n in ("vec0_ld", "vec_ld", "bc_ld", "fin_ld", "stored"))
        consts = sem("consts")
        pv_full, pvt_ps, pvt_done = sem("pv_full"), sem("pvt_ps"), sem("pvt_done")
        pvt0_ps, pvt0_done = sem("pvt0_ps"), sem("pvt0_done")
        x_ready = sem("x_ready")
        xt_ps, tg_done, uh_done, ul_done = sem("xt_ps"), sem("tg_done"), sem("uh_done"), sem("ul_done")
        ssq_done, rs_done = sem("ssq_done"), sem("rs_done")
        gu_t0, sil_done, hid_done, down_t0 = sem("gu_t0"), sem("sil_done"), sem("hid_done"), sem("down_t0")
        ht_ps, hh_done, hl_done, acc_t0 = sem("ht_ps"), sem("hh_done"), sem("hl_done"), sem("acc_t0")
        ct_ps, ct_done, pt_ps, pth_done = sem("ct_ps"), sem("ct_done"), sem("pt_ps"), sem("pth_done")
        ptl_done, hgb_done = sem("ptl_done"), sem("hgb_done")
        ssm_ready, et_ps, et_done = sem("ssm_ready"), sem("et_ps"), sem("et_done")
        kc_ps, kc_done, kc_full, taps_done = sem("kc_ps"), sem("kc_done"), sem("kc_full"), sem("taps_done")
        diag_done, rsb_ps, z_out, u4a_done, u4d_done = (
            sem("diag_done"), sem("rsb_ps"), sem("z_out"), sem("u4a_done"), sem("u4d_done"))
        dl_ps, rot_in, zi_done, scan_done, rot_out, s_done, y_ps = (
            sem("dl_ps"), sem("rot_in"), sem("zi_done"), sem("scan_done"), sem("rot_out"), sem("s_done"), sem("y_ps"))
        conv_done, convd_done, sq_done, sqs_done, st_ps, msy_done, rsy_done = (
            sem("conv_done"), sem("convd_done"), sem("sq_done"), sem("sqs_done"), sem("st_ps"), sem("msy_done"),
            sem("rsy_done"))
        yh_done, yl_done, xa_done = sem("yh_done"), sem("yl_done"), sem("xa_done")
        ysq_done, cub_done, tanh_done, zg_done = sem("ysq_done"), sem("cub_done"), sem("tanh_done"), sem("zg_done")
        zga_done, zgd_done, zgh_done, zgl_done = sem("zga_done"), sem("zgd_done"), sem("zgh_done"), sem("zgl_done")
        glu_h0, th2_done, yy_done = sem("glu_h0"), sem("th2_done"), sem("yy_done")
        pp_done, gate_done, gx_done = sem("pp_done"), sem("gate_done"), sem("gx_done")
        pool_link, dve_link, fin_done, passed = sem("pool_link"), sem("dve_link"), sem("fin_done"), sem("passed")

        PER_SLOT = UNITS // SLOTS
        FFN_BASE = (U_FFN1, U_FFN2)

        def used(l, n):
            return l * UNITS + n + 1 + SLOTS

        def y_at(k, i):
            return i if k == 0 or i < 2 else NCH + i

        block = ctx.enter_context(nc.Block())

        @block.sync
        def _(sp):
            sp.dma_start(xres[:, 0, :], x[0, 0:P, :]).then_inc(x_ld[0], 16)

            def unit(l, n, slot, halves):
                sp.wait_ge(wl_done, l * UNITS + n + 1)
                sp.sem_inc(passed, 1)
                for dst, src in halves:
                    sp.dma_start(dst, src).then_inc(ld[slot], 16)

            def rows(slot, w2d, row):
                v = w2d[bass.ds(row, 2 * P), :].rearrange("(k p) n -> p k n", p=P)
                return [(raw[:, slot, k * D:(k + 1) * D], v[:, k, :]) for k in range(2)]

            def gate_up(slot, wg, wu, col, part):
                dst = raw[:, slot, :].rearrange("p (k g c) -> p k g c", k=4, g=2)
                return [(dst[:, :, g, :], w[part * 512:(part + 1) * 512, bass.ds(col, FC)].rearrange("(k p) c -> p k c", p=P))
                        for g, w in enumerate((wg, wu))]

            def ffn(l, base, wg, wu, wd, then=None):
                for part in range(2):
                    slot = (base + part) % SLOTS
                    unit(l, base + part, slot, gate_up(slot, wg, wu, 0, part))
                if then:
                    then()
                with sp.Fori(1, NFC) as i:
                    for part in range(2):
                        slot = (base - 1 + part) % SLOTS
                        unit(l, i * 3 + (base - 1 + part), slot, gate_up(slot, wg, wu, i * FC, part))
                    slot = (base + 1) % SLOTS
                    unit(l, i * 3 + (base + 1), slot, rows(slot, wd, (i - 1) * FC))
                n = base + 3 * NFC - 1
                unit(l, n, n % SLOTS, rows(n % SLOTS, wd, (NFC - 1) * FC))

            def at(w, l):
                return w[bass.ds(l, 1)].rearrange("o a b -> (o a) b")

            def vec(w, l):
                return w[bass.ds(l, 1)].rearrange("o (k p) -> (o k) p", p=P)

            sp.wait_ge(consts, 1)
            with sp.Fori(0, DEPTH) as l:
                sp.wait_ge(ptl_done, l + 1)
                sp.sem_inc(passed, 1)
                sp.dma_start(pvec0[0:KD, :], vec(ffn1_norm, l)).then_inc(vec0_ld, 16)

                def params():
                    for row, v in ((V_NORM[1], mix_norm), (V_NORM[2], ffn2_norm),
                                   (V_NORM[3], ple_norm), (V_CB, conv_b), (V_GB, glu_b), (V_GA, conv_out_norm),
                                   (V_GS, ssm_out_norm)):
                        sp.dma_start(pvec[row:row + v.shape[1] // P, :], vec(v, l)).then_inc(vec_ld, 16)
                    sp.dma_start(pvec[V_CW:V_CW + 3 * NCH, :],
                                 conv_w[bass.ds(l, 1)].rearrange("o j (k p) -> (o j k) p", p=P)).then_inc(vec_ld, 16)
                    for row, v in ((V_AR, ssm_A_re), (V_AI, ssm_A_im)):
                        sp.dma_start(pvec[row:row + NB, :], v[bass.ds(l, 1)].rearrange("o (b g) p -> (o b) (g p)", g=2)).then_inc(vec_ld, 16)
                    sp.dma_start(ldt[V_LDT:V_LDT + NB, :], ssm_log_dt[bass.ds(l, 1)].rearrange("o (b g) -> (o b) g", g=2)).then_inc(vec_ld, 16)
                    sp.dma_start(pvec[V_D:V_D + NB, 96:128], ssm_D[bass.ds(l, 1)].rearrange("o (b g) h -> (o b) (g h)", g=2)).then_inc(vec_ld, 16)
                    sp.wait_ge(x_ready, l * 16 + 12)
                    sp.sem_inc(passed, 1)
                    sp.dma_start(pnat[:], p[bass.ds(l, 1), 0].rearrange("o (t p) d -> p (o t) d", p=P)).then_inc(bc_ld, 16)
                    for dst, b in ((br, ssm_B_re), (bi, ssm_B_im)):
                        sp.dma_start(dst, b[bass.ds(l, 1)].rearrange("o (b g) p h -> (g p) (o b) h", g=2)).then_inc(bc_ld, 16)
                    for r, c in enumerate((ssm_C_re, ssm_C_im)):
                        for d in range(2):
                            sp.dma_start(cnat[:, r, :, d, :], c[bass.ds(l, 1)].rearrange("o (q g) h p -> (g h) (o q) p", g=8)).then_inc(bc_ld, 16)

                ffn(l, U_FFN1, at(ffn1_w_gate, l), at(ffn1_w_up, l), at(ffn1_w_down, l), params)
                for j in range(8):
                    n = U_IN + j
                    src = at(w_in, l)[:, IN_COLS[j]:IN_COLS[j] + 256].rearrange("(k p) c -> p k c", p=P)
                    dst = raw[:, n % SLOTS, :].rearrange("p (k c) -> p k c", k=KD)
                    unit(l, n, n % SLOTS, [(dst[:, 4 * a:4 * a + 4, :], src[:, 4 * a:4 * a + 4, :]) for a in range(2)])
                unit(l, U_WOUT_A0, U_WOUT_A0 % SLOTS, rows(U_WOUT_A0 % SLOTS, at(w_out, l), 0))
                src = at(glu_w, l).rearrange("(k p) c -> p k c", p=P)
                dst = raw[:, U_GLU % SLOTS, :].rearrange("p (k c) -> p k c", k=NCH)
                unit(l, U_GLU, U_GLU % SLOTS, [(dst[:, 2 * a:2 * a + 2, :], src[:, 2 * a:2 * a + 2, :]) for a in range(2)])
                unit(l, U_WOUT_A1, U_WOUT_A1 % SLOTS, rows(U_WOUT_A1 % SLOTS, at(w_out, l), 2 * P))
                for j in range(2):
                    n = U_WOUT_S + j
                    unit(l, n, n % SLOTS, rows(n % SLOTS, at(w_out, l), CW + j * 2 * P))
                ffn(l, U_FFN2, at(ffn2_w_gate, l), at(ffn2_w_up, l), at(ffn2_w_down, l))
                unit(l, U_PROJ, U_PROJ % SLOTS, rows(U_PROJ % SLOTS, at(ple_w_proj, l), 0))
                for j in range(4):
                    n = U_GATE + j
                    unit(l, n, n % SLOTS, rows(n % SLOTS, at(ple_w_gate, l), j * 2 * P))

            sp.wait_ge(x_ready, DEPTH * 16 + 12)
            sp.dma_start(regT[:, 0:D], final_norm.partition_broadcast(P)).then_inc(fin_ld, 16)
            for q in range(4):
                t, w = q // 2, slice(512 * (q % 2), 512 * (q % 2) + 512)
                sp.wait_ge(fin_done, q + 1)
                sp.dma_start(out[0, t * P:(t + 1) * P, w], xres[:, t, w]).then_inc(stored, 16)
            sp.wait_ge(stored, 16 * 4)

        @block.scalar
        def _(act):
            nc.scalar.preload_act_table_set("silu_and_others")
            act.wait_ge(x_ld[0], 16)
            act.dma_start(xres[:, 1, :], x[0, P:2 * P, :]).then_inc(x_ld[1], 16)

            def split(l, n, slot, load, between=None):
                act.wait_ge(ld[slot], (l * PER_SLOT + load) * 32)
                act.wait_ge(wt_used, l * UNITS + n + 1)
                for a in range(2):
                    if a == 1 and between:
                        between()
                    w = slice(a * UNIT // 2, (a + 1) * UNIT // 2)
                    nc.scalar.activation(wH[:, slot, w], raw[:, slot, w], ACT.Copy).then_inc(wh_done, 1)

            def split_at(l, n, between=None):
                split(l, n, n % SLOTS, n // SLOTS + 1, between)

            def squares(l, m, t):
                act.wait_ge(x_ready, l * 16 + (16 + 4 * m + 2 * t + 2))
                if t == 1:
                    act.wait_ge(ssq_done, l * 8 + (2 * m + 1))
                scratch = regE[:, 0:D] if m == 0 else bufB[:, :]
                nc.scalar.activation(scratch, xres[:, t, :], ACT.Square,
                                     accum_out=ssq[:, t:t + 1]).then_inc(ssq_done, 1)

            def norm_H(l, m, q):
                t, h = q // 2, q % 2
                act.wait_ge(tg_done, l * 16 + (4 * m + q + 1))
                nc.scalar.activation(uH[:, 4 * h:4 * h + 4, t * P:(t + 1) * P],
                                     tg[:, q % 2, :].rearrange("p (k n) -> p k n", k=4),
                                     ACT.Copy).then_inc(uh_done, 1)

            def norm(l, m, first, second):
                split_at(l, first)
                norm_H(l, m, 0)
                norm_H(l, m, 1)
                if m == 1:
                    act.wait_ge(kc_ps, l + 1)
                    nc.scalar.activation(kc[:], ps[:, 7, :].rearrange("p (b c) -> p b c", b=NB), ACT.Copy).then_inc(kc_done, 1)
                    for b in range(4):
                        E_turned(l, 0, b)
                    norm_H(l, m, 2)
                    norm_H(l, m, 3)
                    for b in range(4):
                        E_turned(l, 1, b)
                    squares(l, m, 0)
                    squares(l, m, 1)
                else:
                    squares(l, m, 0)
                    squares(l, m, 1)
                    norm_H(l, m, 2)
                    norm_H(l, m, 3)
                split_at(l, second)

            def E_turned(l, r, b):
                act.wait_ge(et_ps, l * 8 + (4 * r + b + 1))
                nc.scalar.activation((ETr, ETi)[r][:, 4 * b:4 * b + 4, :],
                                     ps[:, SIDE_BANKS[b], :].rearrange("p (b c) -> p b c", b=4),
                                     ACT.Copy).then_inc(et_done, 1)

            def silus(l, f, i, unit_b, between=None):
                for t in range(NT):
                    if t == 1 and between:
                        between()
                    if t == 0:
                        act.wait_ge(gu_t0, l * (2 * NFC) + i + (f * NFC + 1))
                    else:
                        act.wait_ge(wt_used, used(l, unit_b))
                    nc.scalar.activation(sil[:, t, :], ps[:, t, 0:FC], ACT.Silu,
                                         scale=rs[:, t:t + 1]).then_inc(sil_done, 1)

            def hidden_H(l, f, i):
                act.wait_ge(ht_ps, l * (2 * NFC) + i + (f * NFC + 1))
                nc.scalar.activation(hTH[:], ps[:, 6, :].rearrange("p (k n) -> p k n", k=2),
                                     ACT.Copy).then_inc(hh_done, 1)

            def last_hidden_H(l, f):
                act.wait_ge(ht_ps, l * (2 * NFC) + (f + 1) * NFC)
                for t in range(NT):
                    if t == 0:
                        act.wait_ge(down_t0, l * 2 + (f + 1))
                    else:
                        act.wait_ge(wt_used, used(l, FFN_BASE[f] + 3 * NFC - 2))
                        act.wait_ge(hl_done, l * (2 * NFC + 2) + (f + 1) * (NFC + 1) - 1)
                    nc.scalar.activation(hTH[:, :, t * P:(t + 1) * P],
                                         ps[:, 6, :].rearrange("p (k n) -> p k n", k=2)[:, :, t * P:(t + 1) * P],
                                         ACT.Copy).then_inc(hh_done, 1)

            def c_turned(l, r):
                act.wait_ge(ct_ps, l * 2 + (r + 1))
                for g in range(2):
                    src = ps[64 * g:64 * g + 64, 7, :].rearrange("p (b g h) -> p b g h", b=NB, g=2)
                    nc.scalar.activation((cr, nci)[r][64 * g:64 * g + 64], src[:, :, g, :], ACT.Copy,
                                         scale=(1.0, -1.0)[r]).then_inc(ct_done, 1)

            def p_turned(l):
                act.wait_ge(pt_ps, l + 1)
                nc.scalar.activation(pTH[:], ps[:, 7, :].rearrange("p (k n) -> p k n", k=2),
                                     ACT.Copy).then_inc(pth_done, 1)

            def ffn(l, f):
                base = FFN_BASE[f]
                act.wait_ge(rs_done, l * 4 + (2 * f + 1))

                def between():
                    if f == 0:
                        split_at(l, base + 2)
                        act.wait_ge(pvt_ps, l + 1)
                        nc.scalar.activation(pvT[:, KD:P], ps[:, 7, KD:P], ACT.Copy).then_inc(pvt_done, 1)
                    split_at(l, base + 3)

                silus(l, f, 0, base + 1, between)
                if f == 0:
                    c_turned(l, 0)
                    c_turned(l, 1)
                    p_turned(l)
                with act.Fori(1, NFC) as i:
                    hidden_H(l, f, i - 1)
                    for part in range(3):
                        if part == 2:
                            silus(l, f, i, i * 3 + base)
                        u = base + 1 + part
                        split(l, i * 3 + u, u % SLOTS, i + (u // SLOTS + 1))
                last_hidden_H(l, f)

            def split_y(l, k, gain):
                src = (cy, zgT)[k]
                for i in range(NCH):
                    if k == 1 and i % 2 == 0:
                        act.wait_ge(yy_done, l * 2 + (i // 2 + 1))
                    nc.scalar.activation(uH[:, y_at(k, i), :], src[:, i, :], ACT.Copy,
                                         scale=pvT[:, gain + i:gain + i + 1]).then_inc(yh_done, 1)
                nc.scalar.activation(sqy, src, ACT.Square).then_inc(sq_done, 1)

            def mixer(l):
                split_at(l, U_IN + 3)
                act.wait_ge(z_out, l * 8 + 2)
                for s in range(2):
                    for q in range(4):
                        nc.scalar.activation(u4q[32 * s:32 * s + 32, :, q, :], usq[32 * q:32 * q + 32, :, :, s],
                                             ACT.Copy).then_inc(u4a_done, 1)
                split_at(l, U_IN + 4)
                split_at(l, U_IN + 5)

                def place_taps(k):
                    for s in range(T - k):
                        nc.scalar.activation(taps[32 * s:32 * s + 32, :, 32 * (s + k):32 * (s + k) + 32],
                                             kc[32 * (3 - k):32 * (3 - k) + 32], ACT.Copy).then_inc(taps_done, 1)

                act.wait_ge(kc_full, l + 1)
                place_taps(0)
                place_taps(1)
                split_at(l, U_IN + 6)
                place_taps(2)
                place_taps(3)
                act.wait_ge(pvt_done, l + 1)
                nc.scalar.activation(hgb[:], pvT[:, V_GB:V_GB + NCH], ACT.Copy, scale=0.5).then_inc(hgb_done, 1)
                split_at(l, U_IN + 7)
                split_at(l, U_WOUT_A0)
                split_at(l, U_GLU)
                act.wait_ge(z_out, l * 8 + 8)
                split_y(l, 0, V_GA)
                def gelu(h):
                    at = slice(512 * h, 512 * h + 512)
                    act.wait_ge(cub_done, l * 2 + (h + 1))
                    nc.scalar.activation(th[:, at], t1[:, at], ACT.Tanh, scale=GELU_C).then_inc(tanh_done, 1)
                    act.wait_ge(zg_done, l * 2 + (h + 1))
                    i = slice(2 * h, 2 * h + 2)
                    for n in range(ZA):
                        s, q = n // 4, n % 4
                        nc.scalar.activation(zgq[32 * q:32 * q + 32, i, :, s], t1q[32 * s:32 * s + 32, i, q, :],
                                             ACT.Copy, scale=0.5).then_inc(zga_done, 1)

                def y_squares(h):
                    act.wait_ge(y_ps, l * 2 + (h + 1))
                    nc.scalar.activation(t1[:, 512 * h:512 * h + 512], ps[:, 6 + h, :], ACT.Square).then_inc(ysq_done, 1)

                def gelu_H(h):
                    act.wait_ge(zga_done, l * (2 * ZA) + ZA * (h + 1))
                    act.wait_ge(zgd_done, l * (2 * (16 - ZA)) + (16 - ZA) * (h + 1))
                    nc.scalar.activation(uH[:, NCH + 2 * h:NCH + 2 * h + 2, :], zgT[:, 2 * h:2 * h + 2, :],
                                         ACT.Copy).then_inc(zgh_done, 1)

                y_squares(0)
                gelu(0)
                y_squares(1)
                gelu_H(0)
                gelu(1)
                gelu_H(1)
                split_at(l, U_WOUT_A1)
                split_at(l, U_WOUT_S)
                act.wait_ge(hgb_done, l + 1)
                for i in range(NCH):
                    if i == 0:
                        act.wait_ge(glu_h0, l + 1)
                    if i == 2:
                        act.wait_ge(wt_used, used(l, U_GLU))
                    nc.scalar.activation(thv[:, i, :], ps[:, i // 2, (i % 2) * SEQ:(i % 2 + 1) * SEQ], ACT.Tanh,
                                         bias=hgb[:, i:i + 1], scale=0.5).then_inc(th2_done, 1)
                split_y(l, 1, V_GS)
                split_at(l, U_WOUT_S + 1)
                split_at(l, U_FFN2)

            def embedding(l):
                for q in range(4):
                    act.wait_ge(wt_used, used(l, U_PROJ))
                    nc.scalar.activation(pp[:, q // 2, (q % 2) * 512:(q % 2) * 512 + 512],
                                         ps[:, SIDE_BANKS[q], :], ACT.Copy, scale=0.5).then_inc(pp_done, 1)
                split_at(l, U_GATE + 2)
                split_at(l, U_GATE + 3)
                act.wait_ge(rs_done, l * 4 + 4)
                for q in range(4):
                    if q == 0:
                        act.wait_ge(acc_t0, l * 5 + 5)
                    if q == 2:
                        act.wait_ge(wt_used, used(l, U_GATE + 3))
                    if q >= 2:
                        act.wait_ge(gx_done, l * 4 + (q - 1))
                    nc.scalar.activation(bufB[:, (q % 2) * 512:(q % 2) * 512 + 512], ps[:, 2 + q, :], ACT.Tanh,
                                         scale=rs[:, q // 2:q // 2 + 1]).then_inc(gate_done, 1)

            def first_norm(l):
                split_at(l, 0, lambda: norm_H(l, 0, 0))
                norm_H(l, 0, 1)
                split_at(l, 1)
                squares(l, 0, 0)
                squares(l, 0, 1)
                norm_H(l, 0, 2)
                norm_H(l, 0, 3)

            with act.Fori(0, DEPTH) as l:
                act.wait_ge(pvt0_ps, l + 1)
                nc.scalar.activation(pvT[:, 0:KD], ps[:, 7, 0:KD], ACT.Copy).then_inc(pvt0_done, 1)
                first_norm(l)
                ffn(l, 0)
                norm(l, 1, U_IN + 1, U_IN + 2)
                mixer(l)
                norm(l, 2, U_FFN2 + 1, U_FFN2 + 2)
                ffn(l, 1)
                norm(l, 3, U_GATE, U_GATE + 1)
                embedding(l)
            squares(DEPTH, 0, 0)
            squares(DEPTH, 0, 1)

        @block.vector
        def _(dve):
            dve.sem_inc(wl_done, SLOTS)
            dve.sem_inc(ptl_done, 1)
            links = [0]

            def link(l, ins):
                links[0] += 1
                ins.then_inc(dve_link, 1)
                dve.wait_ge(dve_link, l * DVE_LINKS + links[0])

            def split(l, n, slot, between=None):
                for a in range(2):
                    w = slice(a * UNIT // 2, (a + 1) * UNIT // 2)
                    dve.wait_ge(wh_done, l * (2 * UNITS) + n * 2 + (a + 1))
                    nc.vector.tensor_tensor(wL[:, slot, w], raw[:, slot, w], wH[:, slot, w].bitcast(F32),
                                            ALU.subtract).then_inc((wl_half, wl_done)[a], 1)
                    if a == 0 and between:
                        between()

            def split_at(l, n, between=None):
                split(l, n, n % SLOTS, between)

            def gained(l, m, q):
                h = q % 2
                dve.wait_ge(xt_ps, l * 16 + (4 * m + q + 1))
                if q >= 2:
                    dve.wait_ge(ul_done, l * 16 + (4 * m + q - 1))
                g = pvT[:, V_NORM[m] + 4 * h:V_NORM[m] + 4 * h + 4].unsqueeze(2).to_broadcast([P, 4, P])
                nc.vector.tensor_tensor(tg[:, q % 2, :].rearrange("p (k n) -> p k n", k=4),
                                        ps[:, 2 + q, :].rearrange("p (k n) -> p k n", k=4), g,
                                        ALU.mult).then_inc(tg_done, 1)

            def rest(l, m, q):
                t, h = q // 2, q % 2
                dve.wait_ge(uh_done, l * 16 + (4 * m + q + 1))
                at = (slice(None), slice(4 * h, 4 * h + 4), slice(t * P, (t + 1) * P))
                nc.vector.tensor_tensor(uL[at], tg[:, q % 2, :].rearrange("p (k n) -> p k n", k=4),
                                        uH[at].bitcast(F32), ALU.subtract).then_inc(ul_done, 1)

            def half_norm(l, m, t):
                for step in (gained, rest):
                    for h in range(2):
                        step(l, m, 2 * t + h)

            def residual(l, t, banks, scale, ready, count, say):
                dve.wait_ge(ready, count)
                for h in range(2):
                    s = scale if isinstance(scale, float) else scale[:, t:t + 1]
                    at = xres[:, t, 512 * h:512 * h + 512]
                    nc.vector.scalar_tensor_tensor(at, ps[:, banks[2 * t + h], :], s, at, ALU.mult, ALU.add).then_inc(say, 1)

            def into_norm(l, m, banks, scale, acc, unit, first, second):
                residual(l, 0, banks, scale, acc_t0, l * 5 + acc, x_ready)
                if m == 1:
                    dve.wait_ge(pvt_done, l + 1)
                half_norm(l, m, 0)
                residual(l, 1, banks, scale, wt_used, used(l, unit), x_ready)
                if m != 1:
                    split_at(l, first)
                half_norm(l, m, 1)
                if m == 1:
                    split_at(l, first)
                split_at(l, second)

            def hidden(l, f, i, between=None):
                for t in range(NT):
                    if t == 1 and between:
                        between()
                    dve.wait_ge(sil_done, l * (4 * NFC) + i * 2 + (f * 2 * NFC + t + 1))
                    nc.vector.scalar_tensor_tensor(hid[:, t, :], ps[:, t, FC:2 * FC], rs[:, t:t + 1], sil[:, t, :],
                                                   ALU.mult, ALU.mult).then_inc(hid_done, 1)

            def hidden_L(l, f, i):
                dve.wait_ge(hh_done, l * (2 * NFC + 2) + i + (f * (NFC + 1) + 1))
                nc.vector.tensor_tensor(hTL[:], ps[:, 6, :].rearrange("p (k n) -> p k n", k=2),
                                        hTH[:].bitcast(F32), ALU.subtract).then_inc(hl_done, 1)

            def ffn(l, f):
                base = FFN_BASE[f]

                def between():
                    if f == 0:
                        split_at(l, base + 2)
                    split_at(l, base + 3)

                hidden(l, f, 0, between)
                if f == 0:
                    dve.wait_ge(pth_done, l + 1)
                    nc.vector.tensor_tensor(pTL[:], ps[:, 7, :].rearrange("p (k n) -> p k n", k=2),
                                            pTH[:].bitcast(F32), ALU.subtract).then_inc(ptl_done, 1)
                with dve.Fori(1, NFC) as i:
                    hidden_L(l, f, i - 1)
                    for part in range(3):
                        if part == 2:
                            hidden(l, f, i)
                        u = base + 1 + part
                        split(l, i * 3 + u, u % SLOTS)
                for t in range(NT):
                    dve.wait_ge(hh_done, l * (2 * NFC + 2) + (f * (NFC + 1) + NFC + t))
                    nc.vector.tensor_tensor(hTL[:, :, t * P:(t + 1) * P],
                                            ps[:, 6, :].rearrange("p (k n) -> p k n", k=2)[:, :, t * P:(t + 1) * P],
                                            hTH[:, :, t * P:(t + 1) * P].bitcast(F32), ALU.subtract).then_inc(hl_done, 1)

            def two(ap):
                return ap.unsqueeze(1).to_broadcast([P, 2, SEQ])

            def z_evac(l, j):
                dve.wait_ge(wt_used, used(l, U_IN + j))
                src = ps[:, j % 2, :].rearrange("p (i n) -> p i n", i=2)
                i = slice(2 * (j % 2), 2 * (j % 2) + 2)
                if j < 2:
                    dst, other = us[:, i, :], two(rsb[:])
                elif j < 4:
                    dst, other = cy[:, i, :], two(rsb2[:])
                elif j < 6:
                    dst, other = vv[:, i, 2:SEQ + 2], cy[:, i, :]
                else:
                    if j == 6:
                        dve.wait_ge(conv_done, l * 2 + 2)
                    else:
                        dve.wait_ge(convd_done, l * 2 + 2)
                    dst, other = cy[:, i, :], cy[:, i, :]
                nc.vector.tensor_tensor(dst, src, other, ALU.mult).then_inc(z_out, 1)

            def rotate_in(l, h):
                cs = slice(8 * h, 8 * h + 8)
                co, si = cosT[:, cs, :].rearrange("p b c -> p (b c)"), sinT[:, cs, :].rearrange("p b c -> p (b c)")
                if h == 0:
                    dve.wait_ge(dl_ps, l + 1)
                else:
                    dve.wait_ge(s_done, l * 4 + 2)
                re, im = ps[:, 2 + h, :], ps[:, 4 + h, :]
                for n, (a, b) in enumerate(((re, co), (im, si), (im, co), (re, si))):
                    nc.vector.tensor_tensor(mm[:, n, :], a, b, ALU.mult).then_inc(rot_in, 1)
                dve.wait_ge(rot_in, l * 8 + (4 * h + 2))
                link(l, nc.vector.tensor_tensor(zr, mm[:, 0, :], mm[:, 1, :], ALU.add))

            def scan_and_rotate_out(l, h):
                cs = slice(8 * h, 8 * h + 8)
                co, si = cosT[:, cs, :].rearrange("p b c -> p (b c)"), sinT[:, cs, :].rearrange("p b c -> p (b c)")
                de = decay[:, cs, :].rearrange("p b c -> p (b c)")
                nc.vector.tensor_tensor_scan(zr, de, zr, 0.0, ALU.mult, ALU.add).then_inc(scan_done, 1)
                dve.wait_ge(zi_done, l * 2 + (h + 1))
                nc.vector.tensor_tensor_scan(zi, de, zi, 0.0, ALU.mult, ALU.add).then_inc(scan_done, 1)
                dve.wait_ge(scan_done, l * 4 + (2 * h + 2))
                for n, (a, b) in enumerate(((zr, co), (zi, si), (zi, co), (zr, si))):
                    nc.vector.tensor_tensor(mm[:, n, :], a, b, ALU.mult).then_inc(rot_out, 1)

            def rest_y(l, k, gain):
                src = (cy, zgT)[k]
                for i in range(NCH):
                    dve.wait_ge(yh_done, l * 8 + (4 * k + i + 1))
                    nc.vector.scalar_tensor_tensor(uL[:, y_at(k, i), :], src[:, i, :], pvT[:, gain + i:gain + i + 1],
                                                   uH[:, y_at(k, i), :].bitcast(F32), ALU.mult, ALU.subtract).then_inc(yl_done, 1)

            def mean_y(l, k):
                dve.wait_ge(st_ps, l * 2 + (k + 1))
                nc.vector.tensor_scalar(ms_y[:, k, :], ps[:, 2 * k, 0:NT], 1.0 / CW, (EPS, 4 * EPS)[k],
                                        ALU.mult, ALU.add).then_inc(msy_done, 1)

            def conv(l, i):
                cw = lambda j: pvT[:, V_CW + NCH * j + i:V_CW + NCH * j + i + 1]
                o = cy[:, i, :]
                link(l, nc.vector.tensor_scalar(o, vv[:, i, 2:SEQ + 2], cw(2), pvT[:, V_CB + i:V_CB + i + 1],
                                                ALU.mult, ALU.add))
                for j in (1, 0):
                    link(l, nc.vector.scalar_tensor_tensor(o, vv[:, i, j:SEQ + j], cw(j), o, ALU.mult, ALU.add))
                nc.vector.tensor_tensor(o, o, rsb[:], ALU.mult).then_inc(convd_done, 1)

            def mixer(l):
                dve.wait_ge(rs_done, l * 4 + 2)
                for t in range(NT):
                    nc.vector.tensor_scalar(diag[:, t, :], ident[:], rs[:, t:t + 1], None, ALU.mult).then_inc(diag_done, 1)
                dve.wait_ge(rsb_ps, l + 1)
                link(l, nc.vector.tensor_copy(rsb[:], ps[:, 7, 0:SEQ]))
                z_evac(l, 0)
                link(l, nc.vector.tensor_tensor(rsb2[:], rsb[:], rsb[:], ALU.mult))
                split_at(l, U_IN + 3)
                z_evac(l, 1)
                dve.wait_ge(z_out, l * 8 + 2)
                for s in range(2, 4):
                    for q in range(4):
                        nc.vector.tensor_copy(u4q[32 * s:32 * s + 32, :, q, :],
                                              usq[32 * q:32 * q + 32, :, :, s]).then_inc(u4d_done, 1)
                split_at(l, U_IN + 4)
                z_evac(l, 2)
                split_at(l, U_IN + 5)
                rotate_in(l, 0)
                scan_and_rotate_out(l, 0)
                z_evac(l, 3)
                split_at(l, U_IN + 6)
                rotate_in(l, 1)
                dve.wait_ge(z_out, l * 8 + 4)
                z_evac(l, 4)
                scan_and_rotate_out(l, 1)
                split_at(l, U_IN + 7)
                z_evac(l, 5)
                dve.wait_ge(z_out, l * 8 + 6)
                conv(l, 2)
                conv(l, 3)
                split_at(l, U_WOUT_A0)
                z_evac(l, 6)
                z_evac(l, 7)
                split_at(l, U_GLU)
                rest_y(l, 0, V_GA)
                def cubic(h):
                    at = t1[:, 512 * h:512 * h + 512]
                    dve.wait_ge(ysq_done, l * 2 + (h + 1))
                    link(l, nc.vector.tensor_scalar(at, at, 0.044715, 1.0, ALU.mult, ALU.add))
                    nc.vector.tensor_tensor(at, ps[:, 6 + h, :], at, ALU.mult).then_inc(cub_done, 1)

                def gelu(h):
                    at = t1[:, 512 * h:512 * h + 512]
                    dve.wait_ge(tanh_done, l * 2 + (h + 1))
                    nc.vector.scalar_tensor_tensor(at, th[:, 512 * h:512 * h + 512], 1.0,
                                                   ps[:, 6 + h, :], ALU.add, ALU.mult).then_inc(zg_done, 1)
                    dve.wait_ge(zg_done, l * 2 + (h + 1))
                    i = slice(2 * h, 2 * h + 2)
                    for n in range(ZA, 16):
                        s, q = n // 4, n % 4
                        nc.vector.tensor_scalar(zgq[32 * q:32 * q + 32, i, :, s], t1q[32 * s:32 * s + 32, i, q, :],
                                                0.5, None, ALU.mult).then_inc(zgd_done, 1)

                def gelu_L(h):
                    dve.wait_ge(zgh_done, l * 2 + (h + 1))
                    io = slice(NCH + 2 * h, NCH + 2 * h + 2)
                    nc.vector.tensor_tensor(uL[:, io, :], zgT[:, 2 * h:2 * h + 2, :], uH[:, io, :].bitcast(F32),
                                            ALU.subtract).then_inc(zgl_done, 1)

                cubic(0)
                gelu(0)
                cubic(1)
                gelu_L(0)
                mean_y(l, 0)
                gelu(1)
                gelu_L(1)
                split_at(l, U_WOUT_A1)
                split_at(l, U_WOUT_S)
                for h in range(2):
                    dve.wait_ge(th2_done, l * 4 + (2 * h + 2))
                    at = zgT[:, 2 * h:2 * h + 2, :]
                    nc.vector.scalar_tensor_tensor(at, thv[:, 2 * h:2 * h + 2, :], 1.0, at,
                                                   ALU.add, ALU.mult).then_inc(yy_done, 1)
                rest_y(l, 1, V_GS)
                dve.wait_ge(rsy_done, l * 2 + 1)
                residual(l, 0, ACC, rs_y[:, 0, :], acc_t0, l * 5 + 2, xa_done)
                residual(l, 1, ACC, rs_y[:, 0, :], wt_used, used(l, U_WOUT_A1), xa_done)
                split_at(l, U_WOUT_S + 1)
                split_at(l, U_FFN2)
                mean_y(l, 1)
                dve.wait_ge(rsy_done, l * 2 + 2)
                dve.wait_ge(xa_done, l * 4 + 4)

            def embedding(l):
                split_at(l, U_GATE + 2)
                split_at(l, U_GATE + 3)
                for q in range(4):
                    at = bufB[:, (q % 2) * 512:(q % 2) * 512 + 512]
                    t, h = q // 2, q % 2
                    pq = pp[:, t, 512 * h:512 * h + 512]
                    dve.wait_ge(pp_done, l * 4 + (q + 1))
                    dve.wait_ge(gate_done, l * 4 + (q + 1))
                    nc.vector.scalar_tensor_tensor(pq, at, 1.0, pq, ALU.add, ALU.mult).then_inc(gx_done, 1)

            def first_norm(l):
                dve.wait_ge(pvt0_done, l + 1)
                gained(l, 0, 0)
                split_at(l, 0, lambda: rest(l, 0, 0))
                gained(l, 0, 1)
                rest(l, 0, 1)
                split_at(l, 1)
                half_norm(l, 0, 1)

            with dve.Fori(0, DEPTH) as l:
                first_norm(l)
                ffn(l, 0)
                into_norm(l, 1, ACC, 0.5, 1, U_IN - 1, U_IN + 1, U_IN + 2)
                mixer(l)
                into_norm(l, 2, SIDE_BANKS, rs_y[:, 1, :], 3, U_WOUT_S + 1, U_FFN2 + 1, U_FFN2 + 2)
                ffn(l, 1)
                into_norm(l, 3, ACC, 0.5, 4, U_PROJ - 1, U_GATE, U_GATE + 1)
                embedding(l)
            assert links[0] == DVE_LINKS, links
            dve.wait_ge(fin_ld, 16)
            for q in range(4):
                t, w = q // 2, slice(512 * (q % 2), 512 * (q % 2) + 512)
                if q % 2 == 0:
                    dve.wait_ge(rs_done, 4 * DEPTH + (t + 1))
                    dve.wait_ge(xt_ps, 16 * DEPTH)
                nc.vector.scalar_tensor_tensor(xres[:, t, w], xres[:, t, w], rs[:, t:t + 1], regT[:, w],
                                               ALU.mult, ALU.mult).then_inc(fin_done, 1)

        @block.gpsimd
        def _(pool):
            g = nc.gpsimd
            g.memset(pvec0[:], 0.0)
            g.memset(pvec[:], 0.0).then_inc(consts, 1)
            g.memset(ident[:], 0.0).then_inc(consts, 1)
            pool.wait_ge(consts, 2)
            g.affine_select(out=ident[:], in_=ident[:], compare_op=ALU.not_equal, fill=1.0, base=0,
                            pattern=[[-1, P]], channel_multiplier=1).then_inc(consts, 1)
            g.memset(mhalf[:], -0.5).then_inc(consts, 1)
            g.memset(mone[:], -1.0).then_inc(consts, 1)
            for t in range(NCH):
                last = g.memset(vv[:, t, 0:2], 0.0)
            last.then_inc(consts, 1)
            g.memset(ones[:], 1.0).then_inc(consts, 1)
            pool.wait_ge(consts, 7)
            for t in range(NT):
                pool.wait_ge(x_ld[t], 16)
                pool.sem_inc(x_ready, (18, 2)[t])
            links = [0]

            def inv_rms(l, m):
                four = 4.0 if m == 3 else 1.0
                pool.wait_ge(ssq_done, l * 8 + (2 * m + 2))
                pool.sem_inc(passed, 1)
                link(l, g.tensor_scalar(ms[:], ssq[:], four / D, four * EPS, ALU.mult, ALU.add))
                g.tensor_tensor(rs[:], ms[:], mhalf[:, 0:NT], ALU.pow).then_inc(rs_done, 1)

            def link(l, ins):
                links[0] += 1
                ins.then_inc(pool_link, 1)
                pool.wait_ge(pool_link, links[0])

            def setup(l):
                def tt(o, a, b, op):
                    link(l, g.tensor_tensor(o, a, b, op))

                def ts(o, a, s1, s2, op1=ALU.mult, op2=ALU.add):
                    link(l, g.tensor_scalar(o, a, s1, s2, op1, op2))

                v = lambda n: prm[:, n, :]
                (DT, X, N_, R, Q, TMP, EM, E_, PH, SI, CO, CM, NR, NI, LR, MAG, DEN, FR, FI, A2R, A2I, A3R, A3I,
                 A4R, A4I, SHI, CHI, W) = range(28)

                def exp_parts(src):
                    ts(v(X), src, -87.0, 88.0, ALU.max, ALU.min)
                    ts(v(N_), v(X), LOG2E, ROUND)
                    ts(v(N_), v(N_), -ROUND, 1.0, ALU.add, ALU.mult)
                    ts(v(TMP), v(N_), -LN2_HI, 0.0)
                    tt(v(R), v(X), v(TMP), ALU.add)
                    ts(v(TMP), v(N_), -LN2_LO, 0.0)
                    tt(v(R), v(R), v(TMP), ALU.add)
                    ts(v(Q), v(R), 1 / 5040, 1 / 720)
                    for c in (1 / 120, 1 / 24, 1 / 6, 1 / 2, 1.0):
                        tt(v(Q), v(Q), v(R), ALU.mult)
                        ts(v(Q), v(Q), c, 1.0, ALU.add, ALU.mult)
                    tt(v(Q), v(Q), v(R), ALU.mult)
                    ts(prmi[:], v(N_), 127.0, 8388608.0, ALU.add, ALU.mult)
                    pow2 = prmi[:].bitcast(F32)
                    tt(v(Q), v(Q), pow2, ALU.mult)
                    ts(v(EM), pow2, -1.0, 1.0, ALU.add, ALU.mult)
                    tt(v(EM), v(EM), v(Q), ALU.add)
                    tt(v(E_), pow2, v(Q), ALU.add)

                ar, ai = pvT[:, V_AR:V_AR + NB], pvT[:, V_AI:V_AI + NB]
                exp_parts(pvT[:, V_LDT:V_LDT + NB])
                ts(v(TMP), pvT[:, V_LDT:V_LDT + NB], -87.33, 1.0, ALU.is_ge, ALU.mult)
                tt(v(DT), v(E_), v(TMP), ALU.mult)
                tt(v(TMP), ar, v(DT), ALU.mult)
                exp_parts(v(TMP))
                ts(v(MAG), v(EM), 1.0, 1.0, ALU.add, ALU.mult)
                tt(v(PH), ai, v(DT), ALU.mult)
                ts(v(N_), v(PH), 1 / (2 * math.pi), ROUND)
                ts(v(N_), v(N_), -ROUND, 1.0, ALU.add, ALU.mult)
                for c in (TWO_PI_1, TWO_PI_2, TWO_PI_3):
                    ts(v(TMP), v(N_), -c, 0.0)
                    tt(v(PH), v(PH), v(TMP), ALU.add)
                ts(v(PH), v(PH), 0.5, 0.0)
                tt(v(W), v(PH), v(PH), ALU.mult)
                for o, first in ((SHI, 13), (CHI, 14)):
                    ts(v(o), v(W), (-1) ** (first // 2) / math.factorial(first),
                       (-1) ** (first // 2 - 1) / math.factorial(first - 2))
                    for k in range(first - 4, -1, -2):
                        tt(v(o), v(o), v(W), ALU.mult)
                        ts(v(o), v(o), (-1) ** (k // 2) / math.factorial(k), 1.0, ALU.add, ALU.mult)
                tt(v(SHI), v(SHI), v(PH), ALU.mult)
                tt(v(SI), v(SHI), v(CHI), ALU.mult)
                ts(v(SI), v(SI), 2.0, 0.0)
                tt(v(CM), v(SHI), v(SHI), ALU.mult)
                ts(v(CM), v(CM), -2.0, 0.0)
                ts(v(CO), v(CM), 1.0, 1.0, ALU.add, ALU.mult)
                tt(v(NR), v(EM), v(CO), ALU.mult)
                tt(v(NR), v(NR), v(CM), ALU.add)
                tt(v(NI), v(MAG), v(SI), ALU.mult)
                ts(v(LR), v(NR), 1.0, 1.0, ALU.add, ALU.mult)
                tt(v(DEN), ar, ar, ALU.mult)
                tt(v(TMP), ai, ai, ALU.mult)
                tt(v(DEN), v(DEN), v(TMP), ALU.add)
                tt(v(DEN), v(DEN), mone[:], ALU.pow)
                tt(v(FR), v(NR), ar, ALU.mult)
                tt(v(TMP), v(NI), ai, ALU.mult)
                tt(v(FR), v(FR), v(TMP), ALU.add)
                tt(v(FR), v(FR), v(DEN), ALU.mult)
                tt(v(FI), v(NI), ar, ALU.mult)
                tt(v(TMP), v(NR), ai, ALU.mult)
                tt(v(FI), v(FI), v(TMP), ALU.subtract)
                tt(v(FI), v(FI), v(DEN), ALU.mult)

                def cmul(o_r, o_i, a_r, a_i, b_r, b_i, p1, p2):
                    tt(p1, a_r, b_r, ALU.mult)
                    tt(p2, a_i, b_i, ALU.mult)
                    for o, sl in o_r:
                        tt(o, p1[sl], p2[sl], ALU.subtract)
                    tt(p1, a_r, b_i, ALU.mult)
                    tt(p2, a_i, b_r, ALU.mult)
                    for o, sl in o_i:
                        tt(o, p1[sl], p2[sl], ALU.add)

                whole = slice(None)
                for (o_r, o_i), (a_r, a_i), (b_r, b_i) in (((A2R, A2I), (LR, NI), (LR, NI)), ((A3R, A3I), (A2R, A2I), (LR, NI)),
                                                           ((A4R, A4I), (A2R, A2I), (A2R, A2I))):
                    cmul([(v(o_r), whole)], [(v(o_i), whole)], v(a_r), v(a_i), v(b_r), v(b_i), v(TMP), v(W))
                powers = [None, (LR, NI), (A2R, A2I), (A3R, A3I), (A4R, A4I)]

                def tab(c, w=1):
                    return cosT[:, :, c:c + w], sinT[:, :, c:c + w]

                c0, s0 = cosT[:, :, 0], sinT[:, :, 0]
                cmul([(v(Q), whole)], [(v(R), whole)], v(CO), v(SI), v(CO), v(SI), v(TMP), v(W))
                cmul([(c0, whole)], [(s0, whole)], v(Q), v(R), v(Q), v(R), v(TMP), v(W))
                w = 1
                while w < NCK:
                    by = [a.to_broadcast([P, NB, w]) for a in tab(w - 1)]
                    o = tab(w, w)
                    src = tab(0, w)
                    cmul([(o[0], whole)], [(o[1], whole)], src[0], src[1], by[0], by[1], pa[:, :, 0:w], pb[:, :, 0:w])
                    w *= 2
                tt(v(W), v(MAG), v(MAG), ALU.mult)
                tt(v(W), v(W), v(W), ALU.mult)
                g.tensor_copy(decay[:, :, 1:NCK], v(W).unsqueeze(2).to_broadcast([P, NB, NCK - 1])).then_inc(pool_link, 1)
                links[0] += 1
                g.memset(decay[:, :, 0:1], 0.0).then_inc(pool_link, 1)
                links[0] += 1

                pool.wait_ge(bc_ld, (l + 1) * (16 * NBC))
                pool.sem_inc(passed, 1)
                for zeroed in (regE, Gr, Gi, taps):
                    g.memset(zeroed[:], 0.0).then_inc(pool_link, 1)
                    links[0] += 1
                pool.wait_ge(pool_link, links[0])

                def over_h(n):
                    return v(n).unsqueeze(2).to_broadcast([P, NB, GRP])

                def halves(buf, k):
                    return [(buf[64 * q:64 * q + 64, :, k, GRP * q:GRP * q + GRP], slice(64 * q, 64 * q + 64)) for q in range(2)]

                pah, pbh = pa[:, :, 0:GRP], pb[:, :, 0:GRP]
                cmul([(bbr, whole)], [(bbi, whole)], over_h(FR), over_h(FI), br, bi, pah, pbh)
                for o, src in ((Er, bbr), (Ei, bbi)):
                    for part, sl in halves(o, T - 1):
                        link(l, g.tensor_copy(part, src[sl]))
                for k in range(1, T):
                    n_r, n_i = powers[k]
                    cmul(halves(Er, T - 1 - k), halves(Ei, T - 1 - k), over_h(n_r), over_h(n_i), bbr, bbi, pah, pbh)
                pool.wait_ge(ct_done, l * 4 + 4)
                pool.sem_inc(passed, 1)
                for o, src in ((Gr, cr), (Gi, nci)):
                    for part, sl in halves(o, 0):
                        link(l, g.tensor_copy(part, src[sl]))
                for k in range(1, T + 1):
                    n_r, n_i = powers[k]
                    ts(v(W), v(n_i), -1.0, 0.0)
                    cmul(halves(Gr, k), halves(Gi, k), cr, nci, over_h(n_r), over_h(W), pah, pbh)
                pool.wait_ge(pt_ps, l + 1)
                g.tensor_tensor(dtmp[96:128], ident[96:128, 96:128].unsqueeze(1).to_broadcast([32, NB, 32]),
                                pvT[96:128, V_D:V_D + NB].unsqueeze(2).to_broadcast([32, NB, 32]),
                                ALU.mult).then_inc(ssm_ready, 1)
                pool.wait_ge(ssm_ready, l + 1)
                pool.sem_inc(passed, 1)

            def mixer(l):
                pool.wait_ge(rs_done, l * 4 + 2)
                pool.wait_ge(kc_done, l + 1)
                g.tensor_tensor(kc[96:128], kc[96:128], dtmp[96:128], ALU.add).then_inc(kc_full, 1)
                pool.wait_ge(kc_full, l + 1)

                def imag_in(h):
                    pool.wait_ge(rot_in, l * 8 + (4 * h + 4))
                    g.tensor_tensor(zi, mm[:, 2, :], mm[:, 3, :], ALU.subtract).then_inc(zi_done, 1)

                def state(h):
                    pool.wait_ge(rot_out, l * 8 + (4 * h + 4))
                    at = slice(8 * h, 8 * h + 8)
                    g.tensor_tensor(Sr[:, at, :].rearrange("p b c -> p (b c)"), mm[:, 0, :], mm[:, 1, :],
                                    ALU.subtract).then_inc(s_done, 1)
                    g.tensor_tensor(Si[:, at, :].rearrange("p b c -> p (b c)"), mm[:, 2, :], mm[:, 3, :],
                                    ALU.add).then_inc(s_done, 1)

                def conv(i):
                    cw = lambda j: pvT[:, V_CW + NCH * j + i:V_CW + NCH * j + i + 1]
                    o = cy[:, i, :]
                    link(l, g.tensor_scalar(o, vv[:, i, 2:SEQ + 2], cw(2), pvT[:, V_CB + i:V_CB + i + 1], ALU.mult, ALU.add))
                    for j in (1, 0):
                        link(l, g.tensor_scalar(ctmp[:], vv[:, i, j:SEQ + j], cw(j), 0.0, ALU.mult, ALU.add))
                        link(l, g.tensor_tensor(o, o, ctmp[:], ALU.add))
                    g.tensor_tensor(o, o, rsb[:], ALU.mult).then_inc(conv_done, 1)

                imag_in(0)
                state(0)
                imag_in(1)
                pool.wait_ge(z_out, l * 8 + 5)
                pool.sem_inc(passed, 1)
                conv(0)
                state(1)
                pool.wait_ge(conv_done, l * 2 + 1)
                pool.sem_inc(passed, 1)
                conv(1)
                for k in range(2):
                    pool.wait_ge(sq_done, l * 2 + (k + 1))
                    link(l, g.tensor_tensor(sqy[:, 0:2, :], sqy[:, 0:2, :], sqy[:, 2:4, :], ALU.add))
                    g.tensor_tensor(sqy[:, 0, :], sqy[:, 0, :], sqy[:, 1, :], ALU.add).then_inc(sqs_done, 1)
                    pool.wait_ge(msy_done, l * 2 + (k + 1))
                    g.tensor_tensor(rs_y[:, k, :], ms_y[:, k, :], mhalf[:, 0:NT], ALU.pow).then_inc(rsy_done, 1)

            with pool.Fori(0, DEPTH) as l:
                pool.sem_clear(pool_link)
                pool.wait_ge(vec_ld, (l + 1) * (16 * NPV))
                pool.sem_inc(passed, 1)
                g.tensor_copy(pvec[V_LDT:V_LDT + NB, :].rearrange("b (g p) -> b g p", g=2),
                              ldt[V_LDT:V_LDT + NB, :].unsqueeze(2).to_broadcast([NB, 2, ST])).then_inc(pv_full, 1)
                pool.wait_ge(pv_full, l + 1)
                inv_rms(l, 0)
                pool.wait_ge(pvt_done, l + 1)
                pool.sem_inc(passed, 1)
                setup(l)
                inv_rms(l, 1)
                mixer(l)
                inv_rms(l, 2)
                inv_rms(l, 3)
                for q in range(4):
                    pool.wait_ge(gx_done, l * 4 + (q + 1))
                    xq = xres[:, q // 2, (q % 2) * 512:(q % 2) * 512 + 512]
                    g.tensor_tensor(xq, xq, pp[:, q // 2, (q % 2) * 512:(q % 2) * 512 + 512],
                                    ALU.add).then_inc(x_ready, 1)
                pool.wait_ge(x_ready, l * 16 + 36)
                pool.sem_inc(passed, 1)
            for t in range(NT):
                pool.wait_ge(ssq_done, 8 * DEPTH + (t + 1))
                pool.sem_clear(pool_link)
                g.tensor_scalar(ms[:, t:t + 1], ssq[:, t:t + 1], 1.0 / D, EPS, ALU.mult, ALU.add).then_inc(pool_link, 1)
                pool.wait_ge(pool_link, 1)
                g.tensor_tensor(rs[:, t:t + 1], ms[:, t:t + 1], mhalf[:, 0:1], ALU.pow).then_inc(rs_done, 1)

        @block.tensor
        def _(pe):
            mul = nc.tensor.matmul
            pe.sem_inc(wt_used, SLOTS)
            pe.wait_ge(consts, 3)

            def mm3(o, sH, sL, vH, vL, start, stop):
                mul(o, sH, vH, start=start, stop=False)
                mul(o, sH, vL, start=False, stop=False)
                return mul(o, sL, vH, start=False, stop=stop)

            def take(l, n):
                pe.wait_ge(wl_done, l * UNITS + n + (1 + SLOTS))

            def turn_x(l, m, q):
                t, h = q // 2, q % 2
                pe.wait_ge(x_ready, l * 16 + (16 + 4 * m + q + 1))
                for k in range(4):
                    last = nc.tensor.transpose(ps[:, 2 + q, k * P:(k + 1) * P],
                                               xres[:, t, (4 * h + k) * P:(4 * h + k + 1) * P], ident[:])
                last.then_inc(xt_ps, 1)

            def gate_up_tile(slot, part, t, between=None):
                for k in range(4):
                    if k == 2 and between:
                        between()
                    at = (slice(None), 4 * part + k, slice(t * P, (t + 1) * P))
                    w = slice(512 * k, 512 * k + 512)
                    last = mm3(ps[:, t, :], uH[at], uL[at], wH[:, slot, w], wL[:, slot, w],
                               part == 0 and k == 0, part == 1 and k == 3)
                if t == 1:
                    last.then_inc(wt_used, 1)
                elif part == 1:
                    last.then_inc(gu_t0, 1)

            def gate_up(l, n, slot, part):
                take(l, n)
                for t in range(NT):
                    gate_up_tile(slot, part, t)

            def first_gate_up(l, f):
                base = FFN_BASE[f]
                for t in range(NT):
                    for part in range(2):
                        pe.wait_ge(ul_done, l * 16 + (8 * f + 2 * t + part + 1))
                        if t == 0:
                            pe.wait_ge(wl_half, l * UNITS + (base + part + 1))
                        gate_up_tile((base + part) % SLOTS, part, t,
                                     (lambda n=base + part: take(l, n)) if t == 0 else None)
                        if t == 0 and part == 0:
                            turn_x(l, 2 * f, 2)
                            turn_x(l, 2 * f, 3)
                        if t == 1 and part == 0 and f == 0:
                            pe.wait_ge(pv_full, l + 1)
                            pe.wait_ge(pvt0_done, l + 1)
                            nc.tensor.transpose(ps[:, 7, 0:P], pvec[:], ident[:]).then_inc(pvt_ps, 1)

            def rows_tile(slot, sH, sL, k0, banks, t, first, end, beside=()):
                for k in range(2):
                    at = (slice(None), k0 + k, slice(t * P, (t + 1) * P))
                    for h in range(2):
                        w = slice(D * k + 512 * h, D * k + 512 * h + 512)
                        last = mm3(ps[:, banks[2 * t + h], :], sH[at], sL[at], wH[:, slot, w], wL[:, slot, w],
                                   first and k == 0, end and k == 1)
                        for work in beside:
                            if 4 * t + 2 * k + h in work:
                                work[4 * t + 2 * k + h]()
                return last

            def rows2(l, n, sH, sL, k0, banks, first, end, slot=None, say_t0=None, beside=(), between=None):
                slot = n % SLOTS if slot is None else slot
                take(l, n)
                last = rows_tile(slot, sH, sL, k0, banks, 0, first, end, beside)
                if say_t0:
                    last.then_inc(say_t0, 1)
                if between:
                    between()
                rows_tile(slot, sH, sL, k0, banks, 1, first, end, beside).then_inc(wt_used, 1)

            def turn_tile0(l, m):
                q0 = 4 if m == 2 else 5
                return {q0: lambda: turn_x(l, m, 0), q0 + 1: lambda: turn_x(l, m, 1)}

            def down(l, f, i, n, slot, first=False, **more):
                pe.wait_ge(hl_done, l * (2 * NFC + 2) + i + (f * (NFC + 1) + 1))
                rows2(l, n, hTH, hTL, 0, ACC, first, False, slot=slot, **more)

            def last_down(l, f, beside):
                done = l * (2 * NFC + 2) + (f + 1) * (NFC + 1)
                pe.wait_ge(hl_done, done - 1)
                rows2(l, FFN_BASE[f] + 3 * NFC - 1, hTH, hTL, 0, ACC, False, True, say_t0=acc_t0,
                      beside=[beside, turn_tile0(l, 2 * f + 1)], between=lambda: pe.wait_ge(hl_done, done))

            def turn_hidden(l, f, i):
                pe.wait_ge(hid_done, l * (4 * NFC) + i * 2 + (f * 2 * NFC + 2))
                for k in range(2):
                    for t in range(NT):
                        last = nc.tensor.transpose(ps[:, 6, k * SEQ + t * P:k * SEQ + (t + 1) * P],
                                                   hid[:, t, k * P:(k + 1) * P], ident[:])
                last.then_inc(ht_ps, 1)

            def step(l, f, i):
                base = FFN_BASE[f]
                for part in range(2):
                    gate_up(l, i * 3 + (base - 1 + part), (base - 1 + part) % SLOTS, part)
                down(l, f, i - 1, i * 3 + (base + 1), (base + 1) % SLOTS)
                turn_hidden(l, f, i)

            def tap_block(l, b):
                o = ps[:, 7, 32 * b:32 * b + 32]
                mul(o, Er[:, b, :, :].rearrange("p s c -> p (s c)"), Gr[:, b, 0, :], start=True, stop=False)
                last = mul(o, Ei[:, b, :, :].rearrange("p s c -> p (s c)"), Gi[:, b, 0, :], start=False, stop=True)
                if b == NB - 1:
                    last.then_inc(kc_ps, 1)

            def turn_params(l, which):
                if which < 2:
                    if which == 0:
                        pe.wait_ge(pvt_done, l + 1)
                        pe.wait_ge(bc_ld, (l + 1) * (16 * NBC))
                    else:
                        pe.wait_ge(ct_done, l * 4 + 2)
                    for q in range(4):
                        last = nc.tensor.transpose(ps[:, 7, q * P:(q + 1) * P],
                                                   cnat[:, which, q, :, :].rearrange("p d c -> p (d c)"), ident[:])
                    last.then_inc(ct_ps, 1)
                else:
                    pe.wait_ge(ct_done, l * 4 + 4)
                    for k in range(2):
                        for t in range(NT):
                            last = nc.tensor.transpose(ps[:, 7, k * SEQ + t * P:k * SEQ + (t + 1) * P],
                                                       pnat[:, t, k * P:(k + 1) * P], ident[:])
                    last.then_inc(pt_ps, 1)

            def ffn(l, f):
                base = FFN_BASE[f]
                first_gate_up(l, f)
                if f == 0:
                    turn_params(l, 0)
                take(l, base + 2)
                for t in range(NT):
                    pe.wait_ge(hid_done, l * (4 * NFC) + (f * 2 * NFC + t + 1))
                    gate_up_tile((base + 2) % SLOTS, 0, t)
                    if f == 0:
                        turn_params(l, 1 + t)
                turn_hidden(l, f, 0)
                gate_up(l, base + 3, (base + 3) % SLOTS, 1)
                down(l, f, 0, base + 4, (base + 4) % SLOTS, first=True)
                turn_hidden(l, f, 1)
                with pe.Fori(2, NFC - 1) as i:
                    step(l, f, i)
                i = NFC - 1
                for part in range(2):
                    n = base + 3 * i - 1 + part
                    gate_up(l, n, n % SLOTS, part)
                n = base + 3 * i + 1
                taps = [{}, {}]
                if f == 0:
                    pe.wait_ge(ssm_ready, l + 1)
                    pe.wait_ge(ptl_done, l + 2)
                    taps = [{j: lambda b=j: tap_block(l, b) for j in range(8)},
                            {j: lambda b=8 + j: tap_block(l, b) for j in range(8)}]
                down(l, f, i - 1, n, n % SLOTS, say_t0=down_t0, between=lambda: turn_hidden(l, f, i), beside=[taps[0]])
                last_down(l, f, taps[1])

            def w_in_unit(l, j, between=None):
                n = U_IN + j
                take(l, n)
                if j >= 2:
                    pe.wait_ge(z_out, l * 8 + (j - 1))
                w = wH[:, n % SLOTS, :].rearrange("p (k c) -> p k c", k=KD)
                r = wL[:, n % SLOTS, :].rearrange("p (k c) -> p k c", k=KD)
                if j == 0:
                    pe.wait_ge(ul_done, l * 16 + 8)
                if j < 2:
                    pe.wait_ge(et_done, l * 8 + (5 + j))
                for i in range(2):
                    if i == 1 and between:
                        between()
                    for k in range(KD):
                        c = slice(i * P, (i + 1) * P)
                        last = mm3(ps[:, j % 2, i * SEQ:(i + 1) * SEQ], w[:, k, c], r[:, k, c], uH[:, k, :], uL[:, k, :],
                                   k == 0, k == KD - 1)
                last.then_inc(wt_used, 1)

            def turn_E(l, r):
                src = (Er, Ei)[r]
                for b in range(4):
                    if r == 1:
                        pe.wait_ge(et_done, l * 8 + (b + 1))
                    elif b == 3:
                        pe.wait_ge(kc_done, l + 1)
                    for j in range(4):
                        last = nc.tensor.transpose(ps[:, SIDE_BANKS[b], j * P:(j + 1) * P],
                                                   src[:, 4 * b + j, :, :].rearrange("p s c -> p (s c)"), ident[:])
                    last.then_inc(et_ps, 1)

            def stats(l, k):
                pe.wait_ge(sqs_done, l * 2 + (k + 1))
                for t in range(NT):
                    last = mul(ps[:, 2 * k, t:t + 1], sqy[:, 0, t * P:(t + 1) * P], ones[:, 0:1], start=True, stop=True)
                last.then_inc(st_ps, 1)

            def spread_rms(l):
                pe.wait_ge(diag_done, l * 2 + 2)
                pe.wait_ge(et_done, l * 8 + 8)
                for t in range(NT):
                    last = mul(ps[:, 7, t * P:(t + 1) * P], ones[:], diag[:, t, :], start=True, stop=True)
                last.then_inc(rsb_ps, 1)

            def mixer(l):
                turn_E(l, 0)
                turn_x(l, 1, 2)
                turn_x(l, 1, 3)
                turn_E(l, 1)
                w_in_unit(l, 0)
                w_in_unit(l, 1, lambda: spread_rms(l))
                w_in_unit(l, 2)
                pe.wait_ge(u4a_done, l * 8 + 8)
                pe.wait_ge(u4d_done, l * 8 + 8)
                pe.wait_ge(et_done, l * 8 + 8)
                for b in range(NB):
                    c = slice(NCK * (b % 8), NCK * (b % 8) + NCK)
                    mul(ps[:, 2 + b // 8, c], ETr[:, b, :], u4[:, b, :], start=True, stop=True)
                    last = mul(ps[:, 4 + b // 8, c], ETi[:, b, :], u4[:, b, :], start=True, stop=True)
                last.then_inc(dl_ps, 1)
                for j in range(3, 8):
                    w_in_unit(l, j)
                pe.wait_ge(taps_done, l * 10 + 10)
                pe.wait_ge(s_done, l * 4 + 4)
                for b in range(NB):
                    c = NCK * (b % 8)
                    bank = 6 + b // 8
                    gr = Gr[:, b, 1:T + 1, :].rearrange("p k c -> p (k c)")
                    gi = Gi[:, b, 1:T + 1, :].rearrange("p k c -> p (k c)")
                    mul(ps[:, bank, c:c + NCK], taps[:, b, :], u4[:, b, :], start=True, stop=False)
                    mul(ps[:, bank, c + 1:c + NCK], gr, Sr[:, b, 0:NCK - 1], start=False, stop=False)
                    last = mul(ps[:, bank, c + 1:c + NCK], gi, Si[:, b, 0:NCK - 1], start=False, stop=True)
                    if b % 8 == 7:
                        last.then_inc(y_ps, 1)
                pe.wait_ge(z_out, l * 8 + 8)
                stats(l, 0)
                pe.wait_ge(yl_done, l * 8 + 2)
                rows2(l, U_WOUT_A0, uH, uL, 0, ACC, True, False)
                take(l, U_GLU)
                pe.wait_ge(zgl_done, l * 2 + 2)
                pe.wait_ge(msy_done, l * 2 + 1)
                w = wH[:, U_GLU % SLOTS, :].rearrange("p (k c) -> p k c", k=NCH)
                r = wL[:, U_GLU % SLOTS, :].rearrange("p (k c) -> p k c", k=NCH)
                for i in range(NCH):
                    for k in range(NCH):
                        c = slice(i * P, (i + 1) * P)
                        last = mm3(ps[:, i // 2, (i % 2) * SEQ:(i % 2 + 1) * SEQ], w[:, k, c], r[:, k, c],
                                   uH[:, NCH + k, :], uL[:, NCH + k, :], k == 0, k == NCH - 1)
                    if i == 1:
                        last.then_inc(glu_h0, 1)
                last.then_inc(wt_used, 1)
                pe.wait_ge(yl_done, l * 8 + 4)
                rows2(l, U_WOUT_A1, uH, uL, 2, ACC, False, True, say_t0=acc_t0)
                pe.wait_ge(th2_done, l * 4 + 4)
                pe.wait_ge(yl_done, l * 8 + 6)
                rows2(l, U_WOUT_S, uH, uL, 0, SIDE_BANKS, True, False)
                pe.wait_ge(xa_done, l * 4 + 4)
                stats(l, 1)
                pe.wait_ge(yl_done, l * 8 + 8)
                rows2(l, U_WOUT_S + 1, uH, uL, y_at(1, 2), SIDE_BANKS, False, True, say_t0=acc_t0,
                      beside=[turn_tile0(l, 2)])

            def embedding(l):
                rows2(l, U_PROJ, pTH, pTL, 0, SIDE_BANKS, True, True,
                      between=lambda: (turn_x(l, 3, 2), turn_x(l, 3, 3)))
                pe.wait_ge(ul_done, l * 16 + 14)
                rows2(l, U_GATE, uH, uL, 0, ACC, True, False, between=lambda: pe.wait_ge(ul_done, l * 16 + 16))
                rows2(l, U_GATE + 1, uH, uL, 2, ACC, False, False)
                pe.wait_ge(pp_done, l * 4 + 4)
                for t in range(NT):
                    for j in (2, 3):
                        n = U_GATE + j
                        if t == 0:
                            take(l, n)
                        last = rows_tile(n % SLOTS, uH, uL, 2 * j, ACC, t, False, j == 3)
                        if t == 1:
                            last.then_inc(wt_used, 1)
                        elif j == 3:
                            last.then_inc(acc_t0, 1)

            with pe.Fori(0, DEPTH) as l:
                turn_x(l, 0, 0)
                turn_x(l, 0, 1)
                pe.wait_ge(vec0_ld, l * 16 + 16)
                nc.tensor.transpose(ps[:, 7, 0:P], pvec0[:], ident[:]).then_inc(pvt0_ps, 1)
                ffn(l, 0)
                mixer(l)
                ffn(l, 1)
                embedding(l)


_INS = ["x", "p", "ffn1_norm", "ffn1_w_gate", "ffn1_w_up", "ffn1_w_down", "mix_norm", "w_in", "conv_w", "conv_b",
        "ssm_A_re", "ssm_A_im", "ssm_B_re", "ssm_B_im", "ssm_C_re", "ssm_C_im", "ssm_D", "ssm_log_dt", "glu_w",
        "glu_b", "conv_out_norm", "ssm_out_norm", "w_out", "ffn2_norm", "ffn2_w_gate", "ffn2_w_up", "ffn2_w_down",
        "ple_norm", "ple_w_gate", "ple_w_proj", "final_norm"]


def kernel(**inputs):
    import numpy as _np
    import concourse.bacc as _bacc
    from concourse import mybir as _mybir
    from concourse.bass_utils import run_bass_kernel_spmd as _run

    nc = _bacc.Bacc("TRN2", target_bir_lowering=False, num_devices=1)
    arrays, args = {}, []
    for name in _INS:
        a = _np.ascontiguousarray(inputs[name])
        arrays[f"in_{name}_dram"] = a
        args.append(nc.dram_tensor(f"in_{name}_dram", a.shape, _mybir.dt.from_np(a.dtype), kind="ExternalInput").ap())
    args.append(nc.dram_tensor("out_0_dram", (1, SEQ, D), F32, kind="ExternalOutput").ap())
    trunk(nc, *args)
    r = _run(nc, [arrays], core_ids=[0])
    return r.results[0]["out_0_dram"]
```
